# Optimizing a Trainium2 kernel written in Bass

```python
import jax, jax.numpy as jnp
from jax import lax
import numpy as np

D_MODEL = 2048
BATCH = 1
SEQ = 256
DEPTH = 1

CHUNK = 64
D_MIX = D_MODEL
HGRN_WIDTH = D_MIX // 2
HGRN_HEAD_DIM = 128
HGRN_HEADS = HGRN_WIDTH // HGRN_HEAD_DIM
CONV_CH = D_MIX - HGRN_WIDTH
CONV_K = 3
D_FF = 5632
FFN_RESIDUAL_SCALE = 0.5
RMS_EPS = 1e-6
IN_COLS = 4 * HGRN_WIDTH + 3 * CONV_CH

kernel_name = "hgrn2_shortconv_macaron_hybrid"

def rmsnorm(x, w):
    xf = x.astype(jnp.float32)
    y = xf * lax.rsqrt(jnp.mean(xf * xf, axis=-1, keepdims=True) + RMS_EPS)
    return (y * w.astype(jnp.float32)).astype(x.dtype)

def swiglu(h, w_gate, w_up, w_down):
    return (jax.nn.silu(h @ w_gate) * (h @ w_up)) @ w_down

def hgrn2_chunkwise(q, f_logit, i_val, lb):
    bsz, seq, heads, dh = q.shape
    n_chunks = seq // CHUNK
    lb = lb.reshape(heads, dh)
    f = lb + (1.0 - lb) * jax.nn.sigmoid(f_logit)
    log_f = jnp.log(f)
    k = (1.0 - lb) * jax.nn.sigmoid(-f_logit)

    def to_chunks(t):
        return t.reshape(bsz, n_chunks, CHUNK, heads, dh).transpose(1, 0, 3, 2, 4)

    q_c, k_c, v_c, lf_c = to_chunks(q), to_chunks(k), to_chunks(i_val), to_chunks(log_f)
    b = jnp.cumsum(lf_c, axis=3)
    b_last = b[:, :, :, -1:, :]
    q_dec = q_c * jnp.exp(b)
    k_dec = k_c * jnp.exp(-b)
    k_state = k_c * jnp.exp(b_last - b)
    chunk_decay = jnp.exp(b_last[:, :, :, 0, :])

    causal = jnp.tril(jnp.ones((CHUNK, CHUNK), dtype=bool))
    scores = jnp.einsum('nbhck,nbhsk->nbhcs', q_dec, k_dec)
    scores = jnp.where(causal, scores, 0.0)
    o_intra = jnp.einsum('nbhcs,nbhsv->nbhcv', scores, v_c)

    def step(state, inp):
        q_n, k_n, v_n, d_n = inp
        o_n = jnp.einsum('bhck,bhkv->bhcv', q_n, state)
        state = state * d_n[..., None] + jnp.einsum('bhck,bhcv->bhkv', k_n, v_n)
        return state, o_n

    state0 = jnp.zeros((bsz, heads, dh, dh), jnp.float32)
    _, o_inter = lax.scan(step, state0, (q_dec, k_state, v_c, chunk_decay))
    o = o_intra + o_inter
    return o.transpose(1, 0, 3, 2, 4).reshape(bsz, seq, heads, dh)

def causal_depthwise_conv(u, w):
    ch = u.shape[-1]
    rhs = w.reshape(CONV_K, 1, ch).astype(u.dtype)
    return lax.conv_general_dilated(u, rhs, window_strides=(1,), padding=[(CONV_K - 1, 0)],
                                    dimension_numbers=('NWC', 'WIO', 'NWC'), feature_group_count=ch)

def hybrid_mixer(h, w_in, lb, out_norm_w, conv_w, w_out):
    bsz, seq, _ = h.shape
    proj = h @ w_in
    W, C = HGRN_WIDTH, CONV_CH
    q, f_logit, i_val, gate, conv_b, conv_c, conv_h = jnp.split(
        proj, [W, 2 * W, 3 * W, 4 * W, 4 * W + C, 4 * W + 2 * C], axis=-1)

    hs = (bsz, seq, HGRN_HEADS, HGRN_HEAD_DIM)
    o = hgrn2_chunkwise(q.astype(jnp.float32).reshape(hs), f_logit.astype(jnp.float32).reshape(hs),
                        i_val.astype(jnp.float32).reshape(hs), lb)
    o = o * lax.rsqrt(jnp.mean(o * o, axis=-1, keepdims=True) + RMS_EPS)
    o = o * out_norm_w.astype(jnp.float32).reshape(HGRN_HEADS, HGRN_HEAD_DIM)
    o_a = (o.reshape(bsz, seq, W) * jax.nn.silu(gate.astype(jnp.float32))).astype(h.dtype)

    o_b = conv_b * causal_depthwise_conv(conv_c * conv_h, conv_w)

    return jnp.concatenate([o_a, o_b], axis=-1) @ w_out

def setup_inputs(seed: int = 0) -> dict:
    key = jax.random.key(seed)
    ks = jax.random.split(key, 17)
    f32 = jnp.float32

    def dense(k, shape, fan_in):
        return jax.random.normal(k, shape, f32) * (fan_in ** -0.5)

    def gain(k, shape):
        return 1.0 + 0.02 * jax.random.normal(k, shape, f32)

    return {
        "x": jax.random.normal(ks[0], (BATCH, SEQ, D_MODEL), f32),
        "ffn1_norm_w": gain(ks[1], (DEPTH, D_MODEL)),
        "ffn1_w_gate": dense(ks[2], (DEPTH, D_MODEL, D_FF), D_MODEL),
        "ffn1_w_up": dense(ks[3], (DEPTH, D_MODEL, D_FF), D_MODEL),
        "ffn1_w_down": dense(ks[4], (DEPTH, D_FF, D_MODEL), D_FF),
        "mix_norm_w": gain(ks[5], (DEPTH, D_MODEL)),
        "w_in_mix": dense(ks[6], (DEPTH, D_MODEL, IN_COLS), D_MODEL),
        "hgrn_lb_logits": 0.1 * jax.random.normal(ks[7], (DEPTH + 1, HGRN_WIDTH), f32),
        "hgrn_out_norm_w": gain(ks[8], (DEPTH, HGRN_WIDTH)),
        "conv_w": dense(ks[9], (DEPTH, CONV_K, CONV_CH), CONV_K),
        "w_out_mix": dense(ks[10], (DEPTH, D_MIX, D_MODEL), D_MIX),
        "ffn2_norm_w": gain(ks[11], (DEPTH, D_MODEL)),
        "ffn2_w_gate": dense(ks[12], (DEPTH, D_MODEL, D_FF), D_MODEL),
        "ffn2_w_up": dense(ks[13], (DEPTH, D_MODEL, D_FF), D_MODEL),
        "ffn2_w_down": dense(ks[14], (DEPTH, D_FF, D_MODEL), D_FF),
        "final_norm_w": gain(ks[15], (D_MODEL,)),
    }

def reference(x, ffn1_norm_w, ffn1_w_gate, ffn1_w_up, ffn1_w_down, mix_norm_w, w_in_mix,
              hgrn_lb_logits, hgrn_out_norm_w, conv_w, w_out_mix, ffn2_norm_w, ffn2_w_gate,
              ffn2_w_up, ffn2_w_down, final_norm_w):
    lower_bounds = jnp.cumsum(jax.nn.softmax(hgrn_lb_logits.astype(jnp.float32), axis=0), axis=0)
    for l in range(DEPTH):
        x = x + FFN_RESIDUAL_SCALE * swiglu(rmsnorm(x, ffn1_norm_w[l]),
                                            ffn1_w_gate[l], ffn1_w_up[l], ffn1_w_down[l])
        x = x + hybrid_mixer(rmsnorm(x, mix_norm_w[l]), w_in_mix[l], lower_bounds[l],
                             hgrn_out_norm_w[l], conv_w[l], w_out_mix[l])
        x = x + FFN_RESIDUAL_SCALE * swiglu(rmsnorm(x, ffn2_norm_w[l]),
                                            ffn2_w_gate[l], ffn2_w_up[l], ffn2_w_down[l])
    return rmsnorm(x, final_norm_w)


_drawn_inputs = setup_inputs


def setup_inputs(seed=0):
    import zlib

    import numpy as np

    out = dict(_drawn_inputs(seed))
    spreads = {}
    factors = {'ffn1_norm_w': 4.603,
     'hgrn_out_norm_w': 42.631,
     'ffn2_norm_w': 21.65,
     'final_norm_w': 20.866}
    for name, (base, spread) in spreads.items():
        noise = np.random.default_rng([zlib.crc32(name.encode()), seed]).standard_normal(out[name].shape)
        drawn = base * np.exp(spread * noise) if base else spread * noise
        out[name] = __import__('jax').numpy.asarray(drawn.astype(out[name].dtype))
    for name, factor in factors.items():
        out[name] = (out[name] * factor).astype(out[name].dtype)
    return out
```

```python
from contextlib import ExitStack

import concourse.bass as bass
from concourse import mybir

F32 = mybir.dt.float32
F32R = mybir.dt.float32r
U32 = mybir.dt.uint32
ACT = mybir.ActivationFunctionType
ALU = mybir.AluOpType

P = 128
BLK = 512
RING = 4
KB = 2
NB = BLK // P
EPS = 1e-6
CHUNK = 64


def build(nc, x, ffn1_norm_w, ffn1_w_gate, ffn1_w_up, ffn1_w_down, mix_norm_w, w_in_mix, hgrn_lb_logits,
          hgrn_out_norm_w, conv_w, w_out_mix, ffn2_norm_w, ffn2_w_gate, ffn2_w_up, ffn2_w_down, final_norm_w,
          out):
    _, SEQ, D = x.shape
    FF = ffn1_w_gate.shape[2]
    W = hgrn_out_norm_w.shape[1]
    HALVES = SEQ // P
    DK = D // P
    FK = FF // P
    HEADS = W // P
    UN = D // BLK
    FU = FF // BLK
    GL = DK // KB
    DL = FK // KB
    GROUPS = W // BLK
    MU = w_in_mix.shape[2] // BLK
    assert HALVES == 2 and (2 * GL) % RING == 0 and (UN * DL) % RING == 0 and GL == 8 and UN == 4
    assert FF % BLK == 0 and GROUPS == 2 and MU == 14 and SEQ % P == 0 and P == 2 * CHUNK

    T_F1, U_F1, J_F1 = 0, 0, UN
    T_D1, U_D1, J_D1 = T_F1 + 2 * FU * GL, U_F1 + 2 * FU, J_F1 + FU
    T_MX, U_MX, J_MX = T_D1 + UN * DL, U_D1 + UN, J_D1 + UN
    T_OU, U_OU, J_OU = T_MX + MU * GL, U_MX + MU, J_MX + 6 * GROUPS
    T_F2, U_F2, J_F2 = T_OU + UN * GL, U_OU + UN, J_OU + UN
    T_D2, U_D2 = T_F2 + 2 * FU * GL, U_F2 + 2 * FU
    TILES = T_D2 + UN * DL
    N_F1, N_MX, N_F2, N_END = range(4)
    MIX = [(k, g) for g in range(GROUPS) for k in "fqig"] + [(k, g) for g in range(GROUPS) for k in "chb"]
    COL = {"q": 0, "f": W, "i": 2 * W, "g": 3 * W, "b": 4 * W, "c": 4 * W + W, "h": 4 * W + 2 * W}
    TURNED = [m for m in MIX if m[0] != "i"]

    def m_end(kind, g):
        return MIX.index((kind, g)) * GL + GL - 1

    def m_turn(kind, g):
        return J_MX + TURNED.index((kind, g))

    at = [16896]

    def sb(name, shape, dt, offset=None):
        size = 4
        for n in shape[1:]:
            size *= n
        if offset is None:
            offset = at[0]
            at[0] += (size + 31) // 32 * 32
        return nc.alloc_sbuf_tensor_at(name, shape, dt, offset=offset), offset

    raw, _ = sb("raw", [P, RING, KB, BLK], F32)
    whi, _ = sb("whi", [P, RING, KB, BLK], F32R)
    wlo, _ = sb("wlo", [P, RING, KB, BLK], F32R)
    h_hi, hh_at = sb("h_hi", [P, FK, SEQ], F32R)
    h_lo, hl_at = sb("h_lo", [P, FK, SEQ], F32R)
    x_hi, xh_at = sb("x_hi", [P, DK, SEQ], F32R)
    x_lo, xl_at = sb("x_lo", [P, DK, SEQ], F32R)
    res, _ = sb("res", [P, HALVES, D], F32)
    tm, _ = sb("tm", [P, 2, HALVES, BLK], F32)
    junk, _ = sb("junk", [P, BLK], F32)
    ident, _ = sb("ident", [P, P], F32)
    ones, _ = sb("ones", [P, P], F32)
    causal, _ = sb("causal", [P, P], F32)
    restart, _ = sb("restart", [P, NB * SEQ], F32)
    rows, _ = sb("rows", [P, P], F32)
    cols, _ = sb("cols", [P, P], F32)
    ssq, _ = sb("ssq", [P, 4, HALVES, UN], F32)
    ms, _ = sb("ms", [P, 4, HALVES], F32)
    sd, _ = sb("sd", [P, 4, HALVES], F32)
    rstd, _ = sb("rstd", [P, 4, HALVES], F32)
    eps, _ = sb("eps", [P, 1], F32)
    lbw, _ = sb("lbw", [P, 8, HEADS], F32)
    assert at[0] <= 229368

    at[0] = hh_at + DK * SEQ * 4
    kk, _ = sb("kk", [P, NB, SEQ], F32)
    lf, _ = sb("lf", [P, NB, SEQ], F32)
    bc, _ = sb("bc", [P, NB, SEQ], F32)
    kst, _ = sb("kst", [P, NB, SEQ], F32)
    eb, _ = sb("eb", [P, NB, SEQ], F32)
    kdec, _ = sb("kdec", [P, NB, SEQ], F32)
    qdec, _ = sb("qdec", [P, NB, SEQ], F32)
    assert at[0] <= hl_at
    at[0] = hl_at + DK * SEQ * 4
    kst_tm, _ = sb("kst_tm", [P, HALVES, NB, P], F32)
    v_tm, _ = sb("v_tm", [P, HALVES, BLK], F32)
    probs, _ = sb("probs", [P, HALVES, NB, P], F32)
    state, _ = sb("state", [P, 3, NB, P], F32)
    gsil, _ = sb("gsil", [P, NB, SEQ], F32)
    osb, _ = sb("osb", [P, NB, SEQ], F32)
    assert at[0] <= xh_at
    c_sb, u_sb, y_sb, ob = bc, kst, kdec, qdec
    xw, _ = sb("xw", [P, HALVES, D], F32, offset=xh_at)
    fw, _ = sb("fw", [P, D], F32, offset=xl_at)

    C_F1, C_MX, C_F2, C_ON = 0, DK, 2 * DK, 3 * DK
    C_LB, C_CV = 3 * DK + HEADS, 3 * DK + 3 * HEADS
    NROWS = C_CV + 3 * HEADS

    with ExitStack() as ctx:
        acc = [[ctx.enter_context(nc.psum_tensor(f"acc{p}{h}", [P, BLK], F32)) for h in range(2)] for p in range(2)]
        turn = [ctx.enter_context(nc.psum_tensor(f"turn{h}", [P, NB, P], F32)) for h in range(2)]
        xb = [ctx.enter_context(nc.psum_tensor(f"xb{h}", [P, NB, P], F32)) for h in range(2)]

        def sem(name):
            return ctx.enter_context(nc.semaphore(name))

        raw_landed = [sem(f"raw_landed{r}") for r in range(RING)]
        hi_ready = sem("hi_ready")
        lo_ready = sem("lo_ready")
        mm_done = sem("mm_done")
        unit_out = [sem(f"unit_out{p}") for p in range(2)]
        x_landed = [sem(f"x_landed{n}") for n in range(UN)]
        rows_landed = sem("rows_landed")
        fw_landed = sem("fw_landed")
        out_stored = sem("out_stored")
        consts = sem("consts")
        eps_set = sem("eps_set")
        cols_turned = sem("cols_turned")
        cols_ready = sem("cols_ready")
        lb_exp = sem("lb_exp")
        lb_in = sem("lb_in")
        lb_ready = sem("lb_ready")
        turned = sem("turned")
        turn_hi = sem("turn_hi")
        turn_done = sem("turn_done")
        ssq_ready = sem("ssq_ready")
        ms_ready, sd_ready, rstd_ready = sem("ms_ready"), sem("sd_ready"), sem("rstd_ready")
        sig_ready, lf_ready, bc_ready, exp_ready = sem("sig_ready"), sem("lf_ready"), sem("bc_ready"), sem("exp_ready")
        k_ready = sem("k_ready")
        xb_full = sem("xb_full")
        xb_done = sem("xb_done")
        osq_ready, rs_ready, on_ready = sem("osq_ready"), sem("rs_ready"), sem("on_ready")
        oa_ready, oa_hi = sem("oa_ready"), sem("oa_hi")
        mixed = sem("mixed")
        xw_ready = sem("xw_ready")
        y_ready = [sem(f"y_ready{h}") for h in range(HALVES)]
        dve_step = sem("dve_step")

        block = ctx.enter_context(nc.Block())

        X_KST, X_SCORE, X_S12, X_S3, X_O, X_NORM = range(1, 7)

        def xjob(g, kind):
            return 6 * g + kind

        @block.sync
        def _(sp):
            def load(tile, slot, w, rows_at, cols_ap):
                if not isinstance(tile, int) or tile >= RING:
                    sp.wait_ge(lo_ready, tile - RING + 1)
                src = w[0, rows_at:rows_at + KB * P, cols_ap].rearrange("(t p) n -> p t n", p=P)
                sp.dma_start(raw[:, slot], src).then_inc(raw_landed[slot], 16)

            def load_unit(tile0, k0, w, cols_ap, tiles):
                for k in range(tiles):
                    load(tile0 + k0 + k, (k0 + k) % RING, w, k * KB * P, cols_ap)

            def ffn_loads(tile0, gate, up, down):
                load_unit(tile0, 0, gate, slice(0, BLK), GL)
                with sp.Fori(0, FU - 1) as c:
                    load_unit(tile0 + 2 * GL * c, GL, up, bass.ds(c * BLK, BLK), GL)
                    load_unit(tile0 + 2 * GL * c, 2 * GL, gate, bass.ds((c + 1) * BLK, BLK), GL)
                load_unit(tile0, (2 * FU - 1) * GL, up, slice((FU - 1) * BLK, FU * BLK), GL)
                for n in range(UN):
                    load_unit(tile0, 2 * FU * GL + n * DL, down, slice(n * BLK, (n + 1) * BLK), DL)

            for n in range(UN):
                sp.dma_start(res[:, :, n * BLK:(n + 1) * BLK],
                             x[0, :, n * BLK:(n + 1) * BLK].rearrange("(h p) n -> p h n", p=P)).then_inc(x_landed[n], 16)
            ffn_loads(T_F1, ffn1_w_gate, ffn1_w_up, ffn1_w_down)
            for u, (kind, g) in enumerate(MIX):
                c0 = COL[kind] + g * BLK
                load_unit(T_MX, u * GL, w_in_mix, slice(c0, c0 + BLK), GL)
            for n in range(UN):
                load_unit(T_OU, n * GL, w_out_mix, slice(n * BLK, (n + 1) * BLK), GL)
            ffn_loads(T_F2, ffn2_w_gate, ffn2_w_up, ffn2_w_down)

            for h in range(HALVES):
                sp.wait_ge(y_ready[h], 1)
                sp.dma_start(out[0, h * P:(h + 1) * P, :], xw[:, h, :]).then_inc(out_stored, 16)
            sp.wait_ge(out_stored, 16 * HALVES)

        @block.gpsimd
        def _(pool):
            nc.gpsimd.memset(ident[:], 0.0).then_inc(consts, 1)
            pool.wait_ge(consts, 1)
            nc.gpsimd.affine_select(out=ident[:], in_=ident[:], compare_op=ALU.not_equal, fill=1.0, base=0,
                                    pattern=[[-1, P]], channel_multiplier=1).then_inc(consts, 1)
            nc.gpsimd.memset(ones[:], 1.0).then_inc(consts, 1)
            nc.gpsimd.memset(causal[:], 1.0).then_inc(consts, 1)
            pool.wait_ge(consts, 4)
            nc.gpsimd.affine_select(out=causal[:], in_=causal[:], compare_op=ALU.is_ge, fill=0.0, base=0,
                                    pattern=[[1, P]], channel_multiplier=-1).then_inc(consts, 1)
            pool.wait_ge(consts, 5)
            nc.gpsimd.memset(causal[0:CHUNK, CHUNK:P], 0.0).then_inc(consts, 1)
            nc.gpsimd.memset(restart[:], 1.0).then_inc(consts, 1)
            pool.wait_ge(consts, 7)
            nc.gpsimd.memset(restart[:].rearrange("p (n c) -> p n c", c=CHUNK)[:, :, 0:1], 0.0).then_inc(consts, 1)
            pool.wait_ge(mm_done, T_D2)
            pool.dma_start(fw[:], bass.AP(tensor=final_norm_w.tensor, offset=final_norm_w.offset, ap=[[0, P], [1, D]])
                           ).then_inc(fw_landed, 16)

        @block.scalar
        def _(act):
            small = [(C_F1, ffn1_norm_w[0].rearrange("(k p) -> k p", p=P)),
                     (C_MX, mix_norm_w[0].rearrange("(k p) -> k p", p=P)),
                     (C_F2, ffn2_norm_w[0].rearrange("(k p) -> k p", p=P)),
                     (C_ON, hgrn_out_norm_w[0].rearrange("(k p) -> k p", p=P)),
                     (C_LB, hgrn_lb_logits.rearrange("l (k p) -> (l k) p", p=P)),
                     (C_CV, conv_w[0].rearrange("j (k p) -> (j k) p", p=P))]
            for c0, src in small:
                act.dma_start(rows[c0:c0 + src.shape[0], :], src).then_inc(rows_landed, 16)

            def split(tile, slot, lap):
                act.wait_ge(raw_landed[slot], 16 * (lap + 1))
                if not isinstance(tile, int) or tile >= RING:
                    act.wait_ge(mm_done, tile - RING + 1)
                nc.scalar.activation(whi[:, slot], raw[:, slot], ACT.Copy).then_inc(hi_ready, 1)

            def split_at(tile):
                if tile < TILES:
                    split(tile, tile % RING, tile // RING)

            def turn_residual(job, c0, n):
                act.wait_ge(turned, job + 1)
                for j in range(NB):
                    k = n * NB + j
                    both = turn[j // 2][:, 2 * (j % 2):2 * (j % 2) + 2, :].rearrange("p a b -> p (a b)")
                    ins = nc.scalar.activation(x_hi[:, k, :], both,
                                               ACT.Copy, scale=cols[:, c0 + k:c0 + k + 1])
                    if j % 2:
                        ins.then_inc(turn_hi, 1)

            def square(phase, n):
                for h in range(HALVES):
                    before = HALVES * (UN * phase + n) + h
                    if before > 0:
                        act.wait_ge(ssq_ready, before)
                    nc.scalar.activation(junk[:], res[:, h, n * BLK:(n + 1) * BLK], ACT.Square,
                                         accum_out=ssq[:, phase, h, n:n + 1]).then_inc(ssq_ready, 1)

            def root(phase):
                act.wait_ge(ms_ready, phase + 1)
                nc.scalar.activation(sd[:, phase, :], ms[:, phase, :], ACT.Sqrt).then_inc(sd_ready, 1)

            def silu_gate(phase, tile_end, read):
                act.wait_ge(mm_done, tile_end)
                if read is not None:
                    act.wait_ge(unit_out[1], read)
                for h in range(HALVES):
                    ins = nc.scalar.activation(tm[:, 0, h, :], acc[0][h][:], ACT.Silu,
                                               scale=rstd[:, phase, h:h + 1])
                ins.then_inc(unit_out[0], 1)

            def turn_hidden(job, c):
                act.wait_ge(turned, job + 1)
                for h in range(HALVES):
                    ins = nc.scalar.activation(h_hi[:, bass.ds(c * NB, NB), h * P:(h + 1) * P], turn[h][:], ACT.Copy)
                ins.then_inc(turn_hi, 1)

            def lower_bounds():
                act.wait_ge(lb_in, 1)
                nc.scalar.activation(lbw[:, 3:5, :], lbw[:, 1:3, :], ACT.Exp).then_inc(lb_exp, 1)

            def ffn(which, phase, tile0, unit0, job0):
                for s in range(GL):
                    split_at(tile0 + s + RING)
                    if which == 0:
                        if s in (1, 3):
                            turn_residual((s + 3) // 2, C_F1, (s + 3) // 2)
                        if s in (0, 2, 4, 5):
                            n = (0, 2, 4, 5).index(s)
                            act.wait_ge(x_landed[n], 16)
                            square(N_F1, n)
                    elif s == 2:
                        turn_residual(J_F2 - 1, C_F2, UN - 1)
                    if s == 6:
                        root(phase)
                act.wait_ge(rstd_ready, phase + 1)
                silu_gate(phase, tile0 + GL, unit0 // 2 or None)
                with act.Fori(0, FU - 1) as c:
                    for s in range(2 * GL):
                        k = GL + s + RING
                        split(tile0 + 2 * GL * c + k, k % RING, tile0 // RING + 2 * GL // RING * c + k // RING)
                        if s == GL + 2:
                            turn_hidden(job0 + c, c)
                        if s == 2 * GL - 1:
                            silu_gate(phase, tile0 + 2 * GL * c + 3 * GL, unit0 // 2 + c + 1)
                for s in range(GL):
                    split_at(tile0 + (2 * FU - 1) * GL + s + RING)

            def back_to_residual(tiles, tile0, unit0, phase, job0, c_gain, first):
                for s in range(UN * tiles):
                    n, k = s // tiles, s % tiles
                    split_at(tile0 + s + RING)
                    if k == 2 and n == 0:
                        first()
                    if k == 2 and n > 0 and phase != N_END:
                        turn_residual(job0 + n - 1, c_gain, n - 1)
                    if k == tiles - 1:
                        U = unit0 + n
                        act.wait_ge(unit_out[U % 2], U // 2 + 1)
                        square(phase, n)

            def mixer():
                def scaled(u):
                    kind, g = MIX[u]
                    U = U_MX + u
                    act.wait_ge(mm_done, T_MX + (u + 1) * GL)
                    if kind == "i":
                        dst = v_tm
                        if g > 0:
                            act.wait_ge(xb_full, xjob(g - 1, X_O))
                    else:
                        j = TURNED.index((kind, g))
                        dst = tm[:, j % 2]
                        act.wait_ge(turned, J_MX + j - 1)
                    for h in range(HALVES):
                        ins = nc.scalar.activation(dst[:, h, :], acc[U % 2][h][:], ACT.Copy,
                                                   scale=rstd[:, N_MX, h:h + 1])
                        if h == HALVES - 1:
                            ins.then_inc(unit_out[U % 2], 1)

                for s in range(MU * GL):
                    split_at(T_MX + s + RING)
                    if s == 2:
                        turn_residual(J_D1 + UN - 1, C_MX, UN - 1)
                    if s == 5:
                        root(N_MX)
                        act.wait_ge(rstd_ready, N_MX + 1)
                    if s % GL == GL - 1:
                        scaled(s // GL)
                    for g in range(GROUPS):
                        f, q, i, gt = (m_end(kind, g) for kind in "fqig")
                        if s == f + 3:
                            act.wait_ge(turned, m_turn("f", g) + 1)
                            for h in range(HALVES):
                                nc.scalar.activation(lf[:, :, h * P:(h + 1) * P], turn[h][:], ACT.Sigmoid
                                                     ).then_inc(sig_ready, 1)
                            for h in range(HALVES):
                                ins = nc.scalar.activation(kk[:, :, h * P:(h + 1) * P], turn[h][:], ACT.Sigmoid,
                                                           scale=-1.0)
                            ins.then_inc(turn_done, 1)
                            act.wait_ge(sig_ready, HALVES * (g + 1))
                            for j in range(NB):
                                hd = g * NB + j
                                ins = nc.scalar.activation(lf[:, j, :], lf[:, j, :], ACT.Ln,
                                                           scale=lbw[:, 7, hd:hd + 1], bias=lbw[:, 6, hd:hd + 1])
                            ins.then_inc(lf_ready, 1)
                        if s == f + 5:
                            act.wait_ge(bc_ready, 2 * g + 2)
                            nc.scalar.activation(kdec[:], bc[:], ACT.Exp, scale=-1.0)
                            nc.scalar.activation(kst[:], kst[:], ACT.Exp)
                            nc.scalar.activation(eb[:], bc[:], ACT.Exp).then_inc(exp_ready, 1)
                        if s == f + 9:
                            act.wait_ge(xb_full, xjob(g, X_KST))
                            for h in range(HALVES):
                                ins = nc.scalar.activation(kst_tm[:, h], xb[h][:], ACT.Copy)
                            ins.then_inc(xb_done, 1)
                        if s == i + 6:
                            act.wait_ge(xb_done, xjob(g, X_O))
                            nc.scalar.activation(kk[:], osb[:], ACT.Square).then_inc(osq_ready, 1)
                        if s == gt + 1:
                            act.wait_ge(xb_full, xjob(g, X_NORM))
                            for h in range(HALVES):
                                ins = nc.scalar.activation(lf[:, 2 * h:2 * h + 2, :].rearrange("p a b -> p (a b)"),
                                                           xb[h][:].rearrange("p a b -> p (a b)"), ACT.Ln,
                                                           scale=1.0 / P, bias=eps[:, 0:1])
                            ins.then_inc(xb_done, 1)
                            act.wait_ge(xb_done, xjob(g, X_NORM))
                            nc.scalar.activation(lf[:], lf[:], ACT.Exp, scale=-0.5).then_inc(rs_ready, 1)
                        if s == gt + 3:
                            act.wait_ge(turned, m_turn("g", g) + 1)
                            for h in range(HALVES):
                                ins = nc.scalar.activation(gsil[:, :, h * P:(h + 1) * P], turn[h][:], ACT.Silu)
                            ins.then_inc(turn_done, 1)
                        if s == gt + 4:
                            act.wait_ge(oa_ready, g + 1)
                            nc.scalar.activation(h_hi[:, g * NB:(g + 1) * NB, :], osb[:], ACT.Copy).then_inc(oa_hi, 1)
                        c, hh, b = (m_end(kind, g) for kind in "chb")
                        if s == c + 3:
                            act.wait_ge(turned, m_turn("c", g) + 1)
                            for h in range(HALVES):
                                ins = nc.scalar.activation(c_sb[:, :, h * P:(h + 1) * P], turn[h][:], ACT.Copy)
                            ins.then_inc(turn_done, 1)
                        if s == b + 3:
                            conv_hi(g)

            def conv_hi(g):
                act.wait_ge(turn_done, m_turn("b", g) + 1)
                nc.scalar.activation(h_hi[:, HEADS + g * NB:HEADS + (g + 1) * NB, :], ob[:], ACT.Copy
                                     ).then_inc(oa_hi, 1)

            act.wait_ge(cols_ready, 1)
            turn_residual(0, C_F1, 0)
            turn_residual(1, C_F1, 1)
            for t in range(RING):
                split_at(t)
            lower_bounds()
            ffn(0, N_F1, T_F1, U_F1, J_F1)
            back_to_residual(DL, T_D1, U_D1, N_MX, J_D1, C_MX, lambda: turn_hidden(J_F1 + FU - 1, FU - 1))
            act.wait_ge(lb_ready, 1)
            act.wait_ge(eps_set, 1)
            mixer()
            back_to_residual(GL, T_OU, U_OU, N_F2, J_OU, C_F2, lambda: conv_hi(GROUPS - 1))
            ffn(1, N_F2, T_F2, U_F2, J_F2)
            back_to_residual(DL, T_D2, U_D2, N_END, None, None, lambda: turn_hidden(J_F2 + FU - 1, FU - 1))
            root(N_END)
            act.wait_ge(rstd_ready, N_END + 1)
            act.wait_ge(xw_ready, UN)
            nc.scalar.activation(xw[:, 1, :], xw[:, 1, :], ACT.Copy, scale=rstd[:, N_END, 1:2]).then_inc(y_ready[1], 1)

        @block.vector
        def _(dve):
            steps = [0]

            def own(ins):
                steps[0] += 1
                ins.then_inc(dve_step, 1)
                dve.wait_ge(dve_step, steps[0])

            def split(tile, slot):
                dve.wait_ge(hi_ready, tile + 1)
                nc.vector.tensor_tensor(wlo[:, slot], raw[:, slot], whi[:, slot].bitcast(F32), ALU.subtract
                                        ).then_inc(lo_ready, 1)

            def split_at(tile):
                if tile < TILES:
                    split(tile, tile % RING)

            def turn_residual(hi_count, c0, n):
                for j in range(NB):
                    k = n * NB + j
                    if j % 2 == 0:
                        dve.wait_ge(turn_hi, hi_count + j // 2 + 1)
                    ins = nc.vector.scalar_tensor_tensor(
                        x_lo[:, k, :], turn[j // 2][:, 2 * (j % 2):2 * (j % 2) + 2, :].rearrange("p a b -> p (a b)"),
                        cols[:, c0 + k:c0 + k + 1],
                        x_hi[:, k, :].bitcast(F32), ALU.mult, ALU.subtract)
                ins.then_inc(turn_done, 1)

            def mean_square(phase):
                dve.wait_ge(ssq_ready, HALVES * UN * (phase + 1))
                own(nc.vector.reduce_sum(ms[:, phase, :], ssq[:, phase], mybir.AxisListType.X))
                nc.vector.tensor_scalar(ms[:, phase, :], ms[:, phase, :], 1.0 / D, EPS, ALU.mult, ALU.add
                                        ).then_inc(ms_ready, 1)

            def inverse(phase):
                dve.wait_ge(sd_ready, phase + 1)
                nc.vector.reciprocal(rstd[:, phase, :], sd[:, phase, :]).then_inc(rstd_ready, 1)

            def hidden(phase, tile_end, gates):
                dve.wait_ge(mm_done, tile_end)
                dve.wait_ge(unit_out[0], gates)
                for h in range(HALVES):
                    ins = nc.vector.scalar_tensor_tensor(tm[:, 1, h, :], acc[1][h][:], rstd[:, phase, h:h + 1],
                                                         tm[:, 0, h, :], ALU.mult, ALU.mult)
                ins.then_inc(unit_out[1], 1)

            def turn_hidden(hi_count, c):
                dve.wait_ge(turn_hi, hi_count + 1)
                for h in range(HALVES):
                    blocks = bass.ds(c * NB, NB)
                    ins = nc.vector.tensor_tensor(h_lo[:, blocks, h * P:(h + 1) * P], turn[h][:],
                                                  h_hi[:, blocks, h * P:(h + 1) * P].bitcast(F32), ALU.subtract)
                ins.then_inc(turn_done, 1)

            def ffn(which, phase, tile0, unit0, hi0, hi_prev):
                for s in range(GL):
                    split_at(tile0 + s + RING)
                    if which == 0:
                        if s in (1, 3):
                            n = (s + 3) // 2
                            turn_residual(2 * n, C_F1, n)
                    elif s == 2:
                        turn_residual(hi_prev, C_F2, UN - 1)
                    if s == 5:
                        mean_square(phase)
                    if s == 6:
                        inverse(phase)
                with dve.Fori(0, FU - 1) as c:
                    for s in range(2 * GL):
                        k = GL + s + RING
                        split(tile0 + 2 * GL * c + k, k % RING)
                        if s == GL - 1:
                            hidden(phase, tile0 + 2 * GL * c + 2 * GL, unit0 // 2 + c + 1)
                        if s == GL + 2:
                            turn_hidden(hi0 + c, c)
                for s in range(GL):
                    split_at(tile0 + (2 * FU - 1) * GL + s + RING)
                hidden(phase, tile0 + 2 * FU * GL, unit0 // 2 + FU)

            def back_to_residual(tiles, tile0, unit0, phase, scale, hi0, c_gain, first):
                for s in range(UN * tiles):
                    n, k = s // tiles, s % tiles
                    split_at(tile0 + s + RING)
                    if k == 2 and n == 0:
                        first()
                    if k == 2 and n > 0 and phase != N_END:
                        turn_residual(hi0 + 2 * (n - 1), c_gain, n - 1)
                    if k == tiles - 1:
                        U = unit0 + n
                        dve.wait_ge(mm_done, tile0 + s + 1)
                        for h in range(HALVES):
                            part = res[:, h, n * BLK:(n + 1) * BLK]
                            if scale == 1.0:
                                ins = nc.vector.tensor_tensor(part, acc[U % 2][h][:], part, ALU.add)
                            else:
                                ins = nc.vector.scalar_tensor_tensor(part, acc[U % 2][h][:], scale, part,
                                                                     ALU.mult, ALU.add)
                        ins.then_inc(unit_out[U % 2], 1)
                        if phase == N_END:
                            if n == 0:
                                dve.wait_ge(fw_landed, 16)
                            dve.wait_ge(unit_out[U % 2], U // 2 + 1)
                            for h in range(HALVES):
                                cs = slice(n * BLK, (n + 1) * BLK)
                                ins = nc.vector.tensor_tensor(xw[:, h, cs], res[:, h, cs], fw[:, cs], ALU.mult)
                            ins.then_inc(xw_ready, 1)

            def mixer():
                for s in range(MU * GL):
                    split_at(T_MX + s + RING)
                    if s == 2:
                        turn_residual(HI_D1 + 2 * (UN - 1), C_MX, UN - 1)
                    if s == 4:
                        mean_square(N_MX)
                    if s == 5:
                        inverse(N_MX)
                    if s == GL + 1:
                        dve.wait_ge(mm_done, T_MX)
                        own(nc.vector.memset(probs[:], 0.0))
                    for g in range(GROUPS):
                        f, q, i, gt = (m_end(kind, g) for kind in "fqig")
                        if s == f + 4:
                            dve.wait_ge(lf_ready, g + 1)
                            if g == 0:
                                dve.wait_ge(consts, 8)
                            flat = "p a b -> p (a b)"
                            nc.vector.tensor_tensor_scan(bc[:].rearrange(flat), restart[:], lf[:].rearrange(flat), 0.0,
                                                         ALU.mult, ALU.add).then_inc(bc_ready, 1)
                            dve.wait_ge(bc_ready, 2 * g + 1)
                            by_chunk = bc[:].rearrange("p a (n c) -> p (a n) c", c=CHUNK)
                            nc.vector.tensor_tensor(kst[:].rearrange("p a (n c) -> p (a n) c", c=CHUNK),
                                                    by_chunk[:, :, CHUNK - 1:CHUNK].broadcast_to(by_chunk.shape), by_chunk,
                                                    ALU.subtract).then_inc(bc_ready, 1)
                        if s == f + 6:
                            dve.wait_ge(exp_ready, g + 1)
                            for dst in (kst, kdec):
                                for j in range(NB):
                                    hd = g * NB + j
                                    ins = nc.vector.scalar_tensor_tensor(dst[:, j, :], kk[:, j, :], lbw[:, 7, hd:hd + 1],
                                                                         dst[:, j, :], ALU.mult, ALU.mult)
                            ins.then_inc(k_ready, 1)
                        if s == q + 3:
                            dve.wait_ge(turned, m_turn("q", g) + 1)
                            for h in range(HALVES):
                                hs = slice(h * P, (h + 1) * P)
                                ins = nc.vector.tensor_tensor(qdec[:, :, hs], turn[h][:], eb[:, :, hs], ALU.mult)
                            ins.then_inc(turn_done, 1)
                        if s == q + 5:
                            dve.wait_ge(xb_full, xjob(g, X_SCORE))
                            for h in range(HALVES):
                                for j in range(NB):
                                    ins = nc.vector.copy_predicated(probs[:, h, j, :], causal[:].bitcast(U32),
                                                                    xb[h][:, j, :])
                            ins.then_inc(xb_done, 1)
                        if s == i + 2:
                            dve.wait_ge(xb_full, xjob(g, X_S12))
                            own(nc.vector.tensor_copy(state[:, 0], xb[0][:]))
                            for j in range(NB):
                                last = 2 * CHUNK - 1
                                ins = nc.vector.scalar_tensor_tensor(state[:, 1, j, :], state[:, 0, j, :],
                                                                     eb[:, j, last:last + 1], xb[1][:, j, :],
                                                                     ALU.mult, ALU.add)
                            ins.then_inc(xb_done, 1)
                        if s == i + 4:
                            dve.wait_ge(xb_full, xjob(g, X_S3))
                            for j in range(NB):
                                last = 3 * CHUNK - 1
                                ins = nc.vector.scalar_tensor_tensor(state[:, 2, j, :], state[:, 1, j, :],
                                                                     eb[:, j, last:last + 1], xb[0][:, j, :],
                                                                     ALU.mult, ALU.add)
                            ins.then_inc(xb_done, 1)
                        if s == i + 6:
                            dve.wait_ge(xb_full, xjob(g, X_O))
                            for h in range(HALVES):
                                ins = nc.vector.tensor_copy(osb[:, 2 * h:2 * h + 2, :].rearrange("p a b -> p (a b)"),
                                                            xb[h][:].rearrange("p a b -> p (a b)"))
                            ins.then_inc(xb_done, 1)
                        if s == gt + 2:
                            dve.wait_ge(rs_ready, g + 1)
                            for j in range(NB):
                                ins = nc.vector.scalar_tensor_tensor(osb[:, j, :], osb[:, j, :],
                                                                     cols[:, C_ON + g * NB + j:C_ON + g * NB + j + 1],
                                                                     lf[:, j, :], ALU.mult, ALU.mult)
                            ins.then_inc(on_ready, 1)
                        if s == gt + 4:
                            dve.wait_ge(on_ready, g + 1)
                            dve.wait_ge(turn_done, m_turn("g", g) + 1)
                            nc.vector.tensor_tensor(osb[:], osb[:], gsil[:], ALU.mult).then_inc(oa_ready, 1)
                        if s == gt + 5:
                            dve.wait_ge(oa_hi, g + 1)
                            nc.vector.tensor_tensor(h_lo[:, g * NB:(g + 1) * NB, :], osb[:],
                                                    h_hi[:, g * NB:(g + 1) * NB, :].bitcast(F32), ALU.subtract
                                                    ).then_inc(mixed, 1)
                        c, hh, b = (m_end(kind, g) for kind in "chb")
                        if s == hh + 3:
                            dve.wait_ge(turned, m_turn("h", g) + 1)
                            dve.wait_ge(turn_done, m_turn("c", g) + 1)
                            for h in range(HALVES):
                                hs = slice(h * P, (h + 1) * P)
                                ins = nc.vector.tensor_tensor(u_sb[:, :, hs], turn[h][:], c_sb[:, :, hs], ALU.mult)
                            ins.then_inc(turn_done, 1)
                        if s == hh + 4:
                            dve.wait_ge(turn_done, m_turn("h", g) + 1)
                            for back in range(3):
                                for j in range(NB):
                                    k = C_CV + (2 - back) * HEADS + g * NB + j
                                    w1 = cols[:, k:k + 1]
                                    if back == 0:
                                        ins = nc.vector.tensor_scalar(y_sb[:, j, :], u_sb[:, j, :], w1, None, ALU.mult)
                                    else:
                                        ins = nc.vector.scalar_tensor_tensor(
                                            y_sb[:, j, back:SEQ], u_sb[:, j, 0:SEQ - back], w1, y_sb[:, j, back:SEQ],
                                            ALU.mult, ALU.add)
                                own(ins)
                        if s == b + 3:
                            conv_out(g)
                        if s == b + 4:
                            conv_lo(g)

            def conv_out(g):
                dve.wait_ge(turned, m_turn("b", g) + 1)
                for h in range(HALVES):
                    hs = slice(h * P, (h + 1) * P)
                    ins = nc.vector.tensor_tensor(ob[:, :, hs], turn[h][:], y_sb[:, :, hs], ALU.mult)
                ins.then_inc(turn_done, 1)

            def conv_lo(g):
                dve.wait_ge(oa_hi, GROUPS + g + 1)
                ks = slice(HEADS + g * NB, HEADS + (g + 1) * NB)
                nc.vector.tensor_tensor(h_lo[:, ks, :], ob[:], h_hi[:, ks, :].bitcast(F32), ALU.subtract
                                        ).then_inc(mixed, 1)

            nc.vector.memset(eps[:], EPS).then_inc(eps_set, 1)
            dve.wait_ge(cols_turned, 1)
            nc.vector.tensor_copy(cols[:, 0:NROWS], xb[0][:].rearrange("p a b -> p (a b)")[:, 0:NROWS]
                                  ).then_inc(cols_ready, 1)
            turn_residual(0, C_F1, 0)
            turn_residual(2, C_F1, 1)
            for t in range(RING):
                split_at(t)
            dve.wait_ge(cols_ready, 1)
            l0, l1 = cols[:, C_LB:C_LB + HEADS], cols[:, C_LB + HEADS:C_LB + 2 * HEADS]
            own(nc.vector.tensor_tensor(lbw[:, 0, :], l0, l1, ALU.max))
            nc.vector.tensor_tensor(lbw[:, 1, :], l0, lbw[:, 0, :], ALU.subtract)
            nc.vector.tensor_tensor(lbw[:, 2, :], l1, lbw[:, 0, :], ALU.subtract).then_inc(lb_in, 1)
            dve.wait_ge(lb_exp, 1)
            own(nc.vector.tensor_tensor(lbw[:, 0, :], lbw[:, 3, :], lbw[:, 4, :], ALU.add))
            own(nc.vector.reciprocal(lbw[:, 5, :], lbw[:, 0, :]))
            own(nc.vector.tensor_tensor(lbw[:, 6, :], lbw[:, 3, :], lbw[:, 5, :], ALU.mult))
            nc.vector.tensor_scalar(lbw[:, 7, :], lbw[:, 6, :], -1.0, 1.0, ALU.mult, ALU.add).then_inc(lb_ready, 1)

            HI_F1 = 2 * UN
            HI_D1 = HI_F1 + FU
            HI_OU = HI_D1 + 2 * UN
            HI_F2 = HI_OU + 2 * UN
            ffn(0, N_F1, T_F1, U_F1, HI_F1, None)
            back_to_residual(DL, T_D1, U_D1, N_MX, 0.5, HI_D1, C_MX, lambda: turn_hidden(HI_D1 - 1, FU - 1))
            mixer()

            def conv_tail():
                conv_out(GROUPS - 1)
                conv_lo(GROUPS - 1)
            back_to_residual(GL, T_OU, U_OU, N_F2, 1.0, HI_OU, C_F2, conv_tail)
            ffn(1, N_F2, T_F2, U_F2, HI_F2, HI_OU + 2 * (UN - 1))
            back_to_residual(DL, T_D2, U_D2, N_END, 0.5, None, None, lambda: turn_hidden(HI_F2 + FU - 1, FU - 1))
            mean_square(N_END)
            inverse(N_END)
            dve.wait_ge(rstd_ready, N_END + 1)
            dve.wait_ge(xw_ready, UN)
            nc.vector.tensor_scalar(xw[:, 0, :], xw[:, 0, :], rstd[:, N_END, 0:1], None, ALU.mult
                                    ).then_inc(y_ready[0], 1)

        @block.tensor
        def _(pe):
            def products(tile, slot, k0, pair, hi, lo, first, last):
                pe.wait_ge(lo_ready, tile + 1)
                for t in range(KB):
                    for h in range(HALVES):
                        xs = slice(h * P, (h + 1) * P)
                        k = k0 + t
                        one, end = first and t == 0, last and t == KB - 1
                        nc.tensor.matmul(acc[pair][h][:], hi[:, k, xs], whi[:, slot, t, :], start=one, stop=False)
                        nc.tensor.matmul(acc[pair][h][:], hi[:, k, xs], wlo[:, slot, t, :], start=False, stop=False)
                        ins = nc.tensor.matmul(acc[pair][h][:], lo[:, k, xs], whi[:, slot, t, :], start=False, stop=end)
                ins.then_inc(mm_done, 1)

            def turn_tokens(job, unit_pair, count, src):
                pe.wait_ge(turn_done, job)
                pe.wait_ge(unit_out[unit_pair], count)
                for h in range(HALVES):
                    for j in range(NB):
                        ins = nc.tensor.transpose(turn[h][:, j, :], src[:, h, j * P:(j + 1) * P], ident[:])
                ins.then_inc(turned, 1)

            def turn_residual(job, n, U=None):
                if job > 0:
                    pe.wait_ge(turn_done, job)
                if U is None:
                    pe.wait_ge(x_landed[n], 16)
                else:
                    pe.wait_ge(unit_out[U % 2], U // 2 + 1)
                for j in range(NB):
                    for h in range(HALVES):
                        c = n * BLK + j * P
                        ins = nc.tensor.transpose(turn[j // 2][:, 2 * (j % 2) + h, :], res[:, h, c:c + P], ident[:])
                ins.then_inc(turned, 1)

            def ffn(which, tile0, unit0, job0):
                before = unit0 // 2
                if which == 1:
                    for pair in range(2):
                        pe.wait_ge(unit_out[pair], before)
                for s in range(GL):
                    if which == 0 and s % 2 == 0:
                        pe.wait_ge(turn_done, s // 2 + 1)
                    if which == 1 and s == GL - 2:
                        pe.wait_ge(turn_done, J_F2)
                    products(tile0 + s, s % RING, KB * s, 0, x_hi, x_lo, s == 0, s == GL - 1)
                    if which == 0 and s in (1, 3):
                        turn_residual((s + 3) // 2, (s + 3) // 2)
                    if which == 1 and s == 1:
                        turn_residual(J_F2 - 1, UN - 1, U_F2 - 1)
                with pe.Fori(0, FU - 1) as c:
                    for s in range(2 * GL):
                        if s == GL:
                            pe.wait_ge(unit_out[0], before + c + 1)
                        k = s % GL
                        products(tile0 + 2 * GL * c + GL + s, (GL + s) % RING, KB * k, 1 if s < GL else 0, x_hi, x_lo,
                                 k == 0, k == GL - 1)
                        if s == GL + 1:
                            turn_tokens(job0 + c, 1, before + c + 1, tm[:, 1])
                for s in range(GL):
                    products(tile0 + (2 * FU - 1) * GL + s, ((2 * FU - 1) * GL + s) % RING, KB * s, 1, x_hi, x_lo,
                             s == 0, s == GL - 1)

            def back_to_residual(tiles, tile0, unit0, job0, residual, first):
                for s in range(UN * tiles):
                    n, k = s // tiles, s % tiles
                    U = unit0 + n
                    if k == 0:
                        pe.wait_ge(unit_out[U % 2], U // 2)
                    if tiles == GL and n == 0 and k % 2 == 0:
                        pe.wait_ge(mixed, k // 2 + 1)
                    if tiles == DL and n == 0 and k == DL - 2:
                        pe.wait_ge(turn_done, job0)
                    products(tile0 + s, s % RING, KB * k, U % 2, h_hi, h_lo, k == 0, k == tiles - 1)
                    if k == 1 and n == 0:
                        first()
                    if k == 1 and n > 0 and residual:
                        turn_residual(job0 + n - 1, n - 1, U - 1)

            def mixer():
                for s in range(MU * GL):
                    u, k = s // GL, s % GL
                    U = U_MX + u
                    if k == 0:
                        pe.wait_ge(unit_out[U % 2], U // 2)
                    if s == GL - 2:
                        pe.wait_ge(turn_done, J_MX)
                    products(T_MX + s, s % RING, KB * k, U % 2, x_hi, x_lo, k == 0, k == GL - 1)
                    if s == 1:
                        turn_residual(J_MX - 1, UN - 1, U_MX - 1)
                    for kind, g in TURNED:
                        if s == m_end(kind, g) + 2:
                            turn_mixed(kind, g)
                    for g in range(GROUPS):
                        f, q, i, gt = (m_end(kind, g) for kind in "fqig")
                        recurrence(s, g, f, q, i, gt)

            def turn_mixed(kind, g):
                U = U_MX + MIX.index((kind, g))
                turn_tokens(m_turn(kind, g), U % 2, U // 2 + 1, tm[:, TURNED.index((kind, g)) % 2])

            def recurrence(s, g, f, q, i, gt):
                if s == f + 8:
                    if g > 0:
                        pe.wait_ge(xb_done, xjob(g, X_KST) - 1)
                    else:
                        pe.wait_ge(cols_ready, 1)
                    pe.wait_ge(k_ready, g + 1)
                    for h in range(HALVES):
                        for j in range(NB):
                            ins = nc.tensor.transpose(xb[h][:, j, :], kst[:, j, h * P:(h + 1) * P], ident[:])
                    ins.then_inc(xb_full, 1)
                if s == q + 4:
                    pe.wait_ge(xb_done, xjob(g, X_SCORE) - 1)
                    pe.wait_ge(turn_done, m_turn("q", g) + 1)
                    for h in range(HALVES):
                        hs = slice(h * P, (h + 1) * P)
                        for j in range(NB):
                            ins = nc.tensor.matmul(xb[h][:, j, :], kdec[:, j, hs], qdec[:, j, hs], start=True, stop=True)
                    ins.then_inc(xb_full, 1)
                if s == i + 1:
                    pe.wait_ge(xb_done, xjob(g, X_S12) - 1)
                    U = U_MX + MIX.index(("i", g))
                    pe.wait_ge(unit_out[U % 2], U // 2 + 1)
                    for n in range(2):
                        ps = slice(n * CHUNK, (n + 1) * CHUNK)
                        for j in range(NB):
                            ins = nc.tensor.matmul(xb[n][:, j, :], kst_tm[ps, 0, j, :], v_tm[ps, 0, j * P:(j + 1) * P],
                                                   start=True, stop=True)
                    ins.then_inc(xb_full, 1)
                if s == i + 3:
                    pe.wait_ge(xb_done, xjob(g, X_S3) - 1)
                    for j in range(NB):
                        ins = nc.tensor.matmul(xb[0][:, j, :], kst_tm[0:CHUNK, 1, j, :], v_tm[0:CHUNK, 1, j * P:(j + 1) * P],
                                               start=True, stop=True)
                    ins.then_inc(xb_full, 1)
                if s == i + 5:
                    pe.wait_ge(xb_done, xjob(g, X_O) - 1)
                    for j in range(NB):
                        flat = xb[j // 2][:].rearrange("p a b -> p (a b)")
                        for n in range(SEQ // CHUNK):
                            h, cc = n // 2, (n % 2) * CHUNK
                            dst = flat[:, (j % 2) * SEQ + n * CHUNK:(j % 2) * SEQ + (n + 1) * CHUNK]
                            ins = nc.tensor.matmul(dst, v_tm[:, h, j * P:(j + 1) * P], probs[:, h, j, cc:cc + CHUNK],
                                                   start=True, stop=(n == 0))
                            if n > 0:
                                ins = nc.tensor.matmul(dst, state[:, n - 1, j, :], qdec[:, j, n * CHUNK:(n + 1) * CHUNK],
                                                       start=False, stop=True)
                    ins.then_inc(xb_full, 1)
                if s == gt:
                    pe.wait_ge(xb_done, xjob(g, X_NORM) - 1)
                    pe.wait_ge(osq_ready, g + 1)
                    for h in range(HALVES):
                        ins = nc.tensor.matmul(xb[h][:].rearrange("p a b -> p (a b)"), ones[:],
                                               kk[:, 2 * h:2 * h + 2, :].rearrange("p a b -> p (a b)"),
                                               start=True, stop=True)
                    ins.then_inc(xb_full, 1)

            pe.wait_ge(consts, 6)
            pe.wait_ge(rows_landed, 16 * 6)
            nc.tensor.transpose(xb[0][:].rearrange("p a b -> p (a b)")[:, 0:NROWS], rows[0:NROWS, :],
                                ident[0:NROWS, 0:NROWS]).then_inc(cols_turned, 1)
            turn_residual(0, 0)
            turn_residual(1, 1)
            ffn(0, T_F1, U_F1, J_F1)
            back_to_residual(DL, T_D1, U_D1, J_D1, True,
                             lambda: turn_tokens(J_D1 - 1, 1, U_D1 // 2, tm[:, 1]))
            mixer()
            back_to_residual(GL, T_OU, U_OU, J_OU, True, lambda: turn_mixed("b", GROUPS - 1))
            ffn(1, T_F2, U_F2, J_F2)
            back_to_residual(DL, T_D2, U_D2, J_F2 + FU, False,
                             lambda: turn_tokens(J_F2 + FU - 1, 1, U_D2 // 2, tm[:, 1]))


_INS = ["x", "ffn1_norm_w", "ffn1_w_gate", "ffn1_w_up", "ffn1_w_down", "mix_norm_w", "w_in_mix", "hgrn_lb_logits",
        "hgrn_out_norm_w", "conv_w", "w_out_mix", "ffn2_norm_w", "ffn2_w_gate", "ffn2_w_up", "ffn2_w_down",
        "final_norm_w"]


def kernel(**inputs):
    import numpy as _np
    import concourse.bacc as _bacc
    from concourse import mybir as _mybir
    from concourse.bass_utils import run_bass_kernel_spmd as _run

    nc = _bacc.Bacc("TRN2", target_bir_lowering=False, num_devices=1)
    arrays, args = {}, []
    for name in _INS:
        a = _np.ascontiguousarray(inputs[name])
        arrays[f"in_{name}_dram"] = a
        args.append(nc.dram_tensor(f"in_{name}_dram", a.shape, _mybir.dt.from_np(a.dtype), kind="ExternalInput").ap())
    args.append(nc.dram_tensor("out_0_dram", inputs["x"].shape, _mybir.dt.float32, kind="ExternalOutput").ap())
    build(nc, *args)
    r = _run(nc, [arrays], core_ids=[0])
    return r.results[0]["out_0_dram"]
```

```python
from contextlib import ExitStack

import concourse.bass as bass
from concourse import mybir

F32 = mybir.dt.float32
F32R = mybir.dt.float32r
U32 = mybir.dt.uint32
ACT = mybir.ActivationFunctionType
ALU = mybir.AluOpType

P = 128
BLK = 512
RING = 4
KB = 2
NB = BLK // P
EPS = 1e-6
PIECES = 2
CHUNK = 64


def build(nc, x, ffn1_norm_w, ffn1_w_gate, ffn1_w_up, ffn1_w_down, mix_norm_w, w_in_mix, hgrn_lb_logits,
          hgrn_out_norm_w, conv_w, w_out_mix, ffn2_norm_w, ffn2_w_gate, ffn2_w_up, ffn2_w_down, final_norm_w,
          out):
    _, SEQ, D = x.shape
    FF = ffn1_w_gate.shape[2]
    W = hgrn_out_norm_w.shape[1]
    HALVES = SEQ // P
    DK = D // P
    FK = FF // P
    HEADS = W // P
    UN = D // BLK
    FU = FF // BLK
    GL = DK // KB
    DL = FK // KB
    GROUPS = W // BLK
    MU = w_in_mix.shape[2] // BLK
    assert HALVES == 2 and (2 * GL) % RING == 0 and (UN * DL) % RING == 0 and GL == 8 and UN == 4
    assert FF % BLK == 0 and GROUPS == 2 and MU == 14 and SEQ % P == 0 and P == 2 * CHUNK

    T_F1, U_F1, J_F1 = 0, 0, UN
    T_D1, U_D1, J_D1 = T_F1 + 2 * FU * GL, U_F1 + 2 * FU, J_F1 + FU
    T_MX, U_MX, J_MX = T_D1 + UN * DL, U_D1 + UN, J_D1 + UN
    T_OU, U_OU, J_OU = T_MX + MU * GL, U_MX + MU, J_MX + 6 * GROUPS
    T_F2, U_F2, J_F2 = T_OU + UN * GL, U_OU + UN, J_OU + UN
    T_D2, U_D2 = T_F2 + 2 * FU * GL, U_F2 + 2 * FU
    TILES = T_D2 + UN * DL
    N_F1, N_MX, N_F2, N_END = range(4)
    MIX = [(k, g) for g in range(GROUPS) for k in "fqig"] + [(k, g) for g in range(GROUPS) for k in "chb"]
    COL = {"q": 0, "f": W, "i": 2 * W, "g": 3 * W, "b": 4 * W, "c": 4 * W + W, "h": 4 * W + 2 * W}
    TURNED = [m for m in MIX if m[0] != "i"]

    def m_end(kind, g):
        return MIX.index((kind, g)) * GL + GL - 1

    def m_turn(kind, g):
        return J_MX + TURNED.index((kind, g))

    at = [16896]

    def sb(name, shape, dt, offset=None):
        size = 4
        for n in shape[1:]:
            size *= n
        if offset is None:
            offset = at[0]
            at[0] += (size + 31) // 32 * 32
        return nc.alloc_sbuf_tensor_at(name, shape, dt, offset=offset), offset

    raw, _ = sb("raw", [P, RING, KB, BLK], F32)
    whi, _ = sb("whi", [P, RING, KB, BLK], F32R)
    wlo, _ = sb("wlo", [P, RING, KB, BLK], F32R)
    h_hi, hh_at = sb("h_hi", [P, FK, SEQ], F32R)
    h_lo, hl_at = sb("h_lo", [P, FK, SEQ], F32R)
    x_hi, xh_at = sb("x_hi", [P, DK, SEQ], F32R)
    x_lo, xl_at = sb("x_lo", [P, DK, SEQ], F32R)
    res, _ = sb("res", [P, HALVES, D], F32)
    tm, _ = sb("tm", [P, 2, HALVES, BLK], F32)
    junk, _ = sb("junk", [P, BLK], F32)
    ident, _ = sb("ident", [P, P], F32)
    ones, _ = sb("ones", [P, P], F32)
    causal, _ = sb("causal", [P, P], F32)
    restart, _ = sb("restart", [P, NB * SEQ], F32)
    rows, _ = sb("rows", [P, P], F32)
    cols, _ = sb("cols", [P, P], F32)
    ssq, _ = sb("ssq", [P, 4, HALVES, UN], F32)
    ms, _ = sb("ms", [P, 4, HALVES], F32)
    sd, _ = sb("sd", [P, 4, HALVES], F32)
    rstd, _ = sb("rstd", [P, 4, HALVES], F32)
    eps, _ = sb("eps", [P, 1], F32)
    root_warm, _ = sb("root_warm", [P, 1], F32)
    lbw, _ = sb("lbw", [P, 8, HEADS], F32)
    assert at[0] <= 229368

    at[0] = hh_at + DK * SEQ * 4
    kk, _ = sb("kk", [P, NB, SEQ], F32)
    lf, _ = sb("lf", [P, NB, SEQ], F32)
    bc, _ = sb("bc", [P, NB, SEQ], F32)
    kst, _ = sb("kst", [P, NB, SEQ], F32)
    eb, _ = sb("eb", [P, NB, SEQ], F32)
    kdec, _ = sb("kdec", [P, NB, SEQ], F32)
    qdec, _ = sb("qdec", [P, NB, SEQ], F32)
    assert at[0] <= hl_at
    at[0] = hl_at + DK * SEQ * 4
    kst_tm, _ = sb("kst_tm", [P, HALVES, NB, P], F32)
    v_tm, _ = sb("v_tm", [P, HALVES, BLK], F32)
    probs, _ = sb("probs", [P, HALVES, NB, P], F32)
    state, _ = sb("state", [P, 3, NB, P], F32)
    gsil, _ = sb("gsil", [P, NB, SEQ], F32)
    osb, _ = sb("osb", [P, NB, SEQ], F32)
    assert at[0] <= xh_at
    c_sb, u_sb, y_sb, ob = bc, kst, kdec, qdec
    xw, _ = sb("xw", [P, HALVES, D], F32, offset=xh_at)
    fw, _ = sb("fw", [P, D], F32, offset=xl_at)

    C_F1, C_MX, C_F2, C_ON = 0, DK, 2 * DK, 3 * DK
    C_LB, C_CV = 3 * DK + HEADS, 3 * DK + 3 * HEADS
    NROWS = C_CV + 3 * HEADS

    with ExitStack() as ctx:
        acc = [[ctx.enter_context(nc.psum_tensor(f"acc{p}{h}", [P, BLK], F32)) for h in range(2)] for p in range(2)]
        turn = [ctx.enter_context(nc.psum_tensor(f"turn{h}", [P, NB, P], F32)) for h in range(2)]
        xb = [ctx.enter_context(nc.psum_tensor(f"xb{h}", [P, NB, P], F32)) for h in range(2)]

        def sem(name):
            return ctx.enter_context(nc.semaphore(name))

        raw_landed = [sem(f"raw_landed{r}") for r in range(RING)]
        hi_ready = sem("hi_ready")
        lo_ready = sem("lo_ready")
        mm_done = sem("mm_done")
        unit_out = [sem(f"unit_out{p}") for p in range(2)]
        x_landed = [sem(f"x_landed{n}") for n in range(UN)]
        gain_landed = sem("gain_landed")
        rows_landed = sem("rows_landed")
        fw_landed = sem("fw_landed")
        out_stored = sem("out_stored")
        consts = sem("consts")
        eps_set = sem("eps_set")
        cols_turned = sem("cols_turned")
        cols_ready = sem("cols_ready")
        lb_exp = sem("lb_exp")
        lb_in = sem("lb_in")
        lb_ready = sem("lb_ready")
        turned = sem("turned")
        turn_hi = sem("turn_hi")
        warmed = sem("warmed")
        x_pair = sem("x_pair")
        turn_done = sem("turn_done")
        ssq_ready = sem("ssq_ready")
        ms_ready, sd_ready, rstd_ready = sem("ms_ready"), sem("sd_ready"), sem("rstd_ready")
        sig_ready, lf_ready, bc_ready, exp_ready = sem("sig_ready"), sem("lf_ready"), sem("bc_ready"), sem("exp_ready")
        k_ready = sem("k_ready")
        xb_full = sem("xb_full")
        xb_done = sem("xb_done")
        osq_ready, rs_ready, on_ready = sem("osq_ready"), sem("rs_ready"), sem("on_ready")
        oa_ready, oa_hi = sem("oa_ready"), sem("oa_hi")
        mixed = sem("mixed")
        xw_ready = sem("xw_ready")
        half_done = sem("half_done")
        sum_ready = sem("sum_ready")
        y_ready = [sem(f"y_ready{h}") for h in range(HALVES)]
        dve_step = sem("dve_step")

        block = ctx.enter_context(nc.Block())

        X_KST, X_SCORE, X_S12, X_S3, X_O, X_NORM = range(1, 7)

        def xjob(g, kind):
            return 6 * g + kind

        @block.sync
        def _(sp):
            def load(tile, slot, w, rows_at, cols_ap):
                if not isinstance(tile, int) or tile >= RING:
                    sp.wait_ge(lo_ready, tile - RING + 1)
                src = w[0, rows_at:rows_at + KB * P, cols_ap].rearrange("(t p) n -> p t n", p=P)
                sp.dma_start(raw[:, slot], src).then_inc(raw_landed[slot], 16)

            def load_unit(tile0, k0, w, cols_ap, tiles, before={}):
                for k in range(tiles):
                    if k in before:
                        before[k]()
                    load(tile0 + k0 + k, (k0 + k) % RING, w, k * KB * P, cols_ap)

            def ffn_loads(tile0, gate, up, down, before={}):
                load_unit(tile0, 0, gate, slice(0, BLK), GL, before)
                with sp.Fori(0, FU - 1) as c:
                    load_unit(tile0 + 2 * GL * c, GL, up, bass.ds(c * BLK, BLK), GL)
                    load_unit(tile0 + 2 * GL * c, 2 * GL, gate, bass.ds((c + 1) * BLK, BLK), GL)
                load_unit(tile0, (2 * FU - 1) * GL, up, slice((FU - 1) * BLK, FU * BLK), GL)
                for n in range(UN):
                    load_unit(tile0, 2 * FU * GL + n * DL, down, slice(n * BLK, (n + 1) * BLK), DL)

            def load_x(n):
                sp.dma_start(res[:, :, n * BLK:(n + 1) * BLK],
                             x[0, :, n * BLK:(n + 1) * BLK].rearrange("(h p) n -> p h n", p=P)).then_inc(x_landed[n], 16)

            def load_rows():
                small = [(C_MX, mix_norm_w[0].rearrange("(k p) -> k p", p=P)),
                         (C_F2, ffn2_norm_w[0].rearrange("(k p) -> k p", p=P)),
                         (C_ON, hgrn_out_norm_w[0].rearrange("(k p) -> k p", p=P)),
                         (C_LB, hgrn_lb_logits.rearrange("l (k p) -> (l k) p", p=P)),
                         (C_CV, conv_w[0].rearrange("j (k p) -> (j k) p", p=P))]
                for c0, src in small:
                    sp.dma_start(rows[c0:c0 + src.shape[0], :], src).then_inc(rows_landed, 16)

            sp.dma_start(rows[C_F1:C_F1 + DK, :], ffn1_norm_w[0].rearrange("(k p) -> k p", p=P)).then_inc(gain_landed, 16)
            ffn_loads(T_F1, ffn1_w_gate, ffn1_w_up, ffn1_w_down,
                      {0: lambda: load_x(0), 1: lambda: load_x(1), 3: lambda: load_x(2), 4: lambda: load_x(3),
                       5: load_rows})
            for u, (kind, g) in enumerate(MIX):
                c0 = COL[kind] + g * BLK
                load_unit(T_MX, u * GL, w_in_mix, slice(c0, c0 + BLK), GL)
            for n in range(UN):
                load_unit(T_OU, n * GL, w_out_mix, slice(n * BLK, (n + 1) * BLK), GL)
            ffn_loads(T_F2, ffn2_w_gate, ffn2_w_up, ffn2_w_down)

            for piece in range(PIECES):
                cs = slice(piece * D // PIECES, (piece + 1) * D // PIECES)
                for h in range(HALVES):
                    sp.wait_ge(y_ready[h], piece + 1)
                    sp.dma_start(out[0, h * P:(h + 1) * P, cs], xw[:, h, cs]).then_inc(out_stored, 16)
            sp.wait_ge(out_stored, 16 * HALVES * PIECES)

        @block.gpsimd
        def _(pool):
            nc.gpsimd.memset(ident[:], 0.0).then_inc(consts, 1)
            pool.wait_ge(consts, 1)
            nc.gpsimd.affine_select(out=ident[:], in_=ident[:], compare_op=ALU.not_equal, fill=1.0, base=0,
                                    pattern=[[-1, P]], channel_multiplier=1).then_inc(consts, 1)
            nc.gpsimd.memset(ones[:], 1.0).then_inc(consts, 1)
            nc.gpsimd.memset(causal[:], 1.0).then_inc(consts, 1)
            pool.wait_ge(consts, 4)
            nc.gpsimd.affine_select(out=causal[:], in_=causal[:], compare_op=ALU.is_ge, fill=0.0, base=0,
                                    pattern=[[1, P]], channel_multiplier=-1).then_inc(consts, 1)
            pool.wait_ge(consts, 5)
            nc.gpsimd.memset(causal[0:CHUNK, CHUNK:P], 0.0).then_inc(consts, 1)
            nc.gpsimd.memset(restart[:], 1.0).then_inc(consts, 1)
            pool.wait_ge(consts, 7)
            nc.gpsimd.memset(restart[:].rearrange("p (n c) -> p n c", c=CHUNK)[:, :, 0:1], 0.0).then_inc(consts, 1)
            pool.wait_ge(mm_done, T_D2)
            pool.dma_start(fw[:], bass.AP(tensor=final_norm_w.tensor, offset=final_norm_w.offset, ap=[[0, P], [1, D]])
                           ).then_inc(fw_landed, 16)

        @block.scalar
        def _(act):
            act.wait_ge(eps_set, 1)
            nc.scalar.activation(root_warm[:], eps[:], ACT.Sqrt).then_inc(ssq_ready, 1)

            def split(tile, slot, lap):
                act.wait_ge(raw_landed[slot], 16 * (lap + 1))
                if not isinstance(tile, int) or tile >= RING:
                    act.wait_ge(mm_done, tile - RING + 1)
                nc.scalar.activation(whi[:, slot], raw[:, slot], ACT.Copy).then_inc(hi_ready, 1)

            def split_at(tile):
                if tile < TILES:
                    split(tile, tile % RING, tile // RING)

            def turn_residual(job, c0, n, turn=turn):
                act.wait_ge(turned, job + 1)
                for j in range(NB):
                    k = n * NB + j
                    both = turn[j // 2][:, 2 * (j % 2):2 * (j % 2) + 2, :].rearrange("p a b -> p (a b)")
                    ins = nc.scalar.activation(x_hi[:, k, :], both,
                                               ACT.Copy, scale=cols[:, c0 + k:c0 + k + 1])
                    if j % 2:
                        ins.then_inc(turn_hi, 1)

            def square(phase, n):
                for h in range(HALVES):
                    act.wait_ge(ssq_ready, 1 + HALVES * (UN * phase + n) + h)
                    nc.scalar.activation(junk[:], res[:, h, n * BLK:(n + 1) * BLK], ACT.Square,
                                         accum_out=ssq[:, phase, h, n:n + 1]).then_inc(ssq_ready, 1)

            def root(phase):
                act.wait_ge(ms_ready, phase + 1)
                nc.scalar.activation(sd[:, phase, :], ms[:, phase, :], ACT.Sqrt).then_inc(sd_ready, 1)

            def silu_gate(phase, tile_end, read):
                act.wait_ge(mm_done, tile_end)
                if read is not None:
                    act.wait_ge(unit_out[1], read)
                for h in range(HALVES):
                    ins = nc.scalar.activation(tm[:, 0, h, :], acc[0][h][:], ACT.Silu,
                                               scale=rstd[:, phase, h:h + 1])
                ins.then_inc(unit_out[0], 1)

            def turn_hidden(job, c):
                act.wait_ge(turned, job + 1)
                for h in range(HALVES):
                    ins = nc.scalar.activation(h_hi[:, bass.ds(c * NB, NB), h * P:(h + 1) * P], turn[h][:], ACT.Copy)
                ins.then_inc(turn_hi, 1)

            def lower_bounds():
                act.wait_ge(lb_in, 1)
                nc.scalar.activation(lbw[:, 3:5, :], lbw[:, 1:3, :], ACT.Exp).then_inc(lb_exp, 1)

            def ffn(which, phase, tile0, unit0, job0):
                for s in range(GL):
                    split_at(tile0 + s + RING)
                    if which == 0:
                        if s in (1, 3):
                            n = (s + 3) // 2
                            turn_residual(n, C_F1, n, (turn, xb)[n % 2])
                        if s in (0, 2, 4, 5):
                            n = (0, 2, 4, 5).index(s)
                            act.wait_ge(x_landed[n], 16)
                            square(N_F1, n)
                    elif s == 2:
                        turn_residual(J_F2 - 1, C_F2, UN - 1)
                    if s == 6:
                        root(phase)
                act.wait_ge(rstd_ready, phase + 1)
                silu_gate(phase, tile0 + GL, unit0 // 2 or None)
                with act.Fori(0, FU - 1) as c:
                    for s in range(2 * GL):
                        k = GL + s + RING
                        split(tile0 + 2 * GL * c + k, k % RING, tile0 // RING + 2 * GL // RING * c + k // RING)
                        if s == GL + 2:
                            turn_hidden(job0 + c, c)
                        if s == 2 * GL - 1:
                            silu_gate(phase, tile0 + 2 * GL * c + 3 * GL, unit0 // 2 + c + 1)
                for s in range(GL):
                    split_at(tile0 + (2 * FU - 1) * GL + s + RING)

            def back_to_residual(tiles, tile0, unit0, phase, job0, c_gain, first):
                for s in range(UN * tiles):
                    n, k = s // tiles, s % tiles
                    split_at(tile0 + s + RING)
                    if k == 2 and n == 0:
                        first()
                    if k == 2 and n > 0 and phase != N_END:
                        turn_residual(job0 + n - 1, c_gain, n - 1)
                    if k == 3 and n == 0 and phase == N_END:
                        act.wait_ge(ssq_ready, 1)
                        nc.scalar.activation(root_warm[:], eps[:], ACT.Sqrt)
                    if k == tiles - 1 and (phase != N_END or n < UN - 1):
                        U = unit0 + n
                        act.wait_ge(unit_out[U % 2], U // 2 + 1)
                        square(phase, n)

            def mixer():
                def scaled(u):
                    kind, g = MIX[u]
                    U = U_MX + u
                    act.wait_ge(mm_done, T_MX + (u + 1) * GL)
                    if kind == "i":
                        dst = v_tm
                        if g > 0:
                            act.wait_ge(xb_full, xjob(g - 1, X_O))
                    else:
                        j = TURNED.index((kind, g))
                        dst = tm[:, j % 2]
                        act.wait_ge(turned, J_MX + j - 1)
                    for h in range(HALVES):
                        ins = nc.scalar.activation(dst[:, h, :], acc[U % 2][h][:], ACT.Copy,
                                                   scale=rstd[:, N_MX, h:h + 1])
                        if h == HALVES - 1:
                            ins.then_inc(unit_out[U % 2], 1)

                for s in range(MU * GL):
                    if s % GL == GL - 1:
                        scaled(s // GL)
                    split_at(T_MX + s + RING)
                    if s == 2:
                        turn_residual(J_D1 + UN - 1, C_MX, UN - 1)
                    if s == 5:
                        root(N_MX)
                        act.wait_ge(rstd_ready, N_MX + 1)
                    for g in range(GROUPS):
                        f, q, i, gt = (m_end(kind, g) for kind in "fqig")
                        if s == f + 3:
                            act.wait_ge(turned, m_turn("f", g) + 1)
                            for h in range(HALVES):
                                nc.scalar.activation(lf[:, :, h * P:(h + 1) * P], turn[h][:], ACT.Sigmoid
                                                     ).then_inc(sig_ready, 1)
                            for h in range(HALVES):
                                ins = nc.scalar.activation(kk[:, :, h * P:(h + 1) * P], turn[h][:], ACT.Sigmoid,
                                                           scale=-1.0)
                            ins.then_inc(turn_done, 1)
                        if s == f + 4:
                            act.wait_ge(sig_ready, HALVES * (g + 1))
                            for j in range(NB):
                                hd = g * NB + j
                                ins = nc.scalar.activation(lf[:, j, :], lf[:, j, :], ACT.Ln,
                                                           scale=lbw[:, 7, hd:hd + 1], bias=lbw[:, 6, hd:hd + 1])
                            ins.then_inc(lf_ready, 1)
                        if s == f + 6:
                            act.wait_ge(bc_ready, 2 * g + 2)
                            nc.scalar.activation(kst[:], kst[:], ACT.Exp).then_inc(exp_ready, 1)
                        if s == f + 7:
                            nc.scalar.activation(kdec[:], bc[:], ACT.Exp, scale=-1.0).then_inc(exp_ready, 1)
                        if s == f + 8:
                            nc.scalar.activation(eb[:], bc[:], ACT.Exp).then_inc(exp_ready, 1)
                        if s == f + 13:
                            act.wait_ge(xb_full, xjob(g, X_KST))
                            for h in range(HALVES):
                                ins = nc.scalar.activation(kst_tm[:, h], xb[h][:], ACT.Copy)
                            ins.then_inc(xb_done, 1)
                        if s == i + 9:
                            act.wait_ge(xb_done, xjob(g, X_O))
                            nc.scalar.activation(kk[:], osb[:], ACT.Square).then_inc(osq_ready, 1)
                        if s == gt + 4:
                            act.wait_ge(xb_full, xjob(g, X_NORM))
                            for h in range(HALVES):
                                ins = nc.scalar.activation(lf[:, 2 * h:2 * h + 2, :].rearrange("p a b -> p (a b)"),
                                                           xb[h][:].rearrange("p a b -> p (a b)"), ACT.Ln,
                                                           scale=1.0 / P, bias=eps[:, 0:1])
                            ins.then_inc(xb_done, 1)
                            act.wait_ge(xb_done, xjob(g, X_NORM))
                            nc.scalar.activation(lf[:], lf[:], ACT.Exp, scale=-0.5).then_inc(rs_ready, 1)
                        if s == gt + 3:
                            act.wait_ge(turned, m_turn("g", g) + 1)
                            for h in range(HALVES):
                                ins = nc.scalar.activation(gsil[:, :, h * P:(h + 1) * P], turn[h][:], ACT.Silu)
                            ins.then_inc(turn_done, 1)
                        if s == gt + 7:
                            act.wait_ge(oa_ready, g + 1)
                            nc.scalar.activation(h_hi[:, g * NB:(g + 1) * NB, :], osb[:], ACT.Copy).then_inc(oa_hi, 1)
                        c, hh, b = (m_end(kind, g) for kind in "chb")
                        if s == c + 3:
                            act.wait_ge(turned, m_turn("c", g) + 1)
                            for h in range(HALVES):
                                ins = nc.scalar.activation(c_sb[:, :, h * P:(h + 1) * P], turn[h][:], ACT.Copy)
                            ins.then_inc(turn_done, 1)
                        if s == b + 3:
                            conv_hi(g)

            def conv_hi(g):
                act.wait_ge(turn_done, m_turn("b", g) + 1)
                nc.scalar.activation(h_hi[:, HEADS + g * NB:HEADS + (g + 1) * NB, :], ob[:], ACT.Copy
                                     ).then_inc(oa_hi, 1)

            act.wait_ge(cols_ready, 1)
            split_at(0)
            turn_residual(0, C_F1, 0)
            split_at(1)
            turn_residual(1, C_F1, 1, xb)
            split_at(2)
            split_at(3)
            ffn(0, N_F1, T_F1, U_F1, J_F1)
            lower_bounds()
            back_to_residual(DL, T_D1, U_D1, N_MX, J_D1, C_MX, lambda: turn_hidden(J_F1 + FU - 1, FU - 1))
            act.wait_ge(lb_ready, 1)
            mixer()
            back_to_residual(GL, T_OU, U_OU, N_F2, J_OU, C_F2, lambda: conv_hi(GROUPS - 1))
            ffn(1, N_F2, T_F2, U_F2, J_F2)
            back_to_residual(DL, T_D2, U_D2, N_END, None, None, lambda: turn_hidden(J_F2 + FU - 1, FU - 1))
            n = UN - 1
            for h in range(HALVES):
                act.wait_ge(sum_ready, h + 1)
                act.wait_ge(ssq_ready, 1 + HALVES * (UN * N_END + n) + h)
                nc.scalar.activation(junk[:], res[:, h, n * BLK:(n + 1) * BLK], ACT.Square,
                                     accum_out=ssq[:, N_END, h, n:n + 1]).then_inc(ssq_ready, 1)
            for h in range(HALVES):
                act.wait_ge(ms_ready, N_END + 1 + h)
                nc.scalar.activation(sd[:, N_END, h:h + 1], ms[:, N_END, h:h + 1], ACT.Sqrt).then_inc(sd_ready, 1)
            act.wait_ge(rstd_ready, N_END + 2)
            act.wait_ge(xw_ready, UN + 1)
            for piece in range(PIECES):
                cs = slice(piece * D // PIECES, (piece + 1) * D // PIECES)
                nc.scalar.activation(xw[:, 1, cs], xw[:, 1, cs], ACT.Copy, scale=rstd[:, N_END, 1:2]
                                     ).then_inc(y_ready[1], 1)

        @block.vector
        def _(dve):
            steps = [0]

            def own(ins):
                steps[0] += 1
                ins.then_inc(dve_step, 1)
                dve.wait_ge(dve_step, steps[0])

            def split(tile, slot):
                dve.wait_ge(hi_ready, tile + 1)
                nc.vector.tensor_tensor(wlo[:, slot], raw[:, slot], whi[:, slot].bitcast(F32), ALU.subtract
                                        ).then_inc(lo_ready, 1)

            def split_at(tile):
                if tile < TILES:
                    split(tile, tile % RING)

            def turn_residual(hi_count, c0, n, turn=turn):
                for j in range(NB):
                    k = n * NB + j
                    if j % 2 == 0:
                        dve.wait_ge(turn_hi, hi_count + j // 2 + 1)
                    ins = nc.vector.scalar_tensor_tensor(
                        x_lo[:, k, :], turn[j // 2][:, 2 * (j % 2):2 * (j % 2) + 2, :].rearrange("p a b -> p (a b)"),
                        cols[:, c0 + k:c0 + k + 1],
                        x_hi[:, k, :].bitcast(F32), ALU.mult, ALU.subtract)
                    if c0 == C_F1 and j == KB - 1:
                        ins.then_inc(x_pair, 1)
                ins.then_inc(turn_done, 1)

            def mean_square(phase):
                dve.wait_ge(ssq_ready, 1 + HALVES * UN * (phase + 1))
                own(nc.vector.reduce_sum(ms[:, phase, :], ssq[:, phase], mybir.AxisListType.X))
                nc.vector.tensor_scalar(ms[:, phase, :], ms[:, phase, :], 1.0 / D, EPS, ALU.mult, ALU.add
                                        ).then_inc(ms_ready, 1)

            def inverse(phase):
                dve.wait_ge(sd_ready, phase + 1)
                nc.vector.reciprocal(rstd[:, phase, :], sd[:, phase, :]).then_inc(rstd_ready, 1)

            def hidden(phase, tile_end, gates):
                dve.wait_ge(mm_done, tile_end)
                dve.wait_ge(unit_out[0], gates)
                for h in range(HALVES):
                    ins = nc.vector.scalar_tensor_tensor(tm[:, 1, h, :], acc[1][h][:], rstd[:, phase, h:h + 1],
                                                         tm[:, 0, h, :], ALU.mult, ALU.mult)
                ins.then_inc(unit_out[1], 1)

            def turn_hidden(hi_count, c):
                dve.wait_ge(turn_hi, hi_count + 1)
                for h in range(HALVES):
                    blocks = bass.ds(c * NB, NB)
                    ins = nc.vector.tensor_tensor(h_lo[:, blocks, h * P:(h + 1) * P], turn[h][:],
                                                  h_hi[:, blocks, h * P:(h + 1) * P].bitcast(F32), ALU.subtract)
                ins.then_inc(turn_done, 1)

            def ffn(which, phase, tile0, unit0, hi0, hi_prev):
                for s in range(GL):
                    split_at(tile0 + s + RING)
                    if which == 0:
                        if s in (1, 3):
                            n = (s + 3) // 2
                            turn_residual(2 * n, C_F1, n, (turn, xb)[n % 2])
                    elif s == 2:
                        turn_residual(hi_prev, C_F2, UN - 1)
                    if s == 5:
                        mean_square(phase)
                    if s == 6:
                        inverse(phase)
                        if which == 0:
                            other_columns()
                with dve.Fori(0, FU - 1) as c:
                    for s in range(2 * GL):
                        k = GL + s + RING
                        split(tile0 + 2 * GL * c + k, k % RING)
                        if s == GL - 1:
                            hidden(phase, tile0 + 2 * GL * c + 2 * GL, unit0 // 2 + c + 1)
                        if s == GL + 2:
                            turn_hidden(hi0 + c, c)
                for s in range(GL):
                    split_at(tile0 + (2 * FU - 1) * GL + s + RING)
                hidden(phase, tile0 + 2 * FU * GL, unit0 // 2 + FU)

            def back_to_residual(tiles, tile0, unit0, phase, scale, hi0, c_gain, first):
                for s in range(UN * tiles):
                    n, k = s // tiles, s % tiles
                    split_at(tile0 + s + RING)
                    if k == 2 and n == 0:
                        first()
                    if k == 2 and n > 0 and phase != N_END:
                        turn_residual(hi0 + 2 * (n - 1), c_gain, n - 1)
                    if k == tiles - 1 and (phase != N_END or n < UN - 1):
                        U = unit0 + n
                        dve.wait_ge(mm_done, tile0 + s + 1)
                        for h in range(HALVES):
                            part = res[:, h, n * BLK:(n + 1) * BLK]
                            if scale == 1.0:
                                ins = nc.vector.tensor_tensor(part, acc[U % 2][h][:], part, ALU.add)
                            else:
                                ins = nc.vector.scalar_tensor_tensor(part, acc[U % 2][h][:], scale, part,
                                                                     ALU.mult, ALU.add)
                        ins.then_inc(unit_out[U % 2], 1)
                        if phase == N_END:
                            if n == 0:
                                dve.wait_ge(fw_landed, 16)
                            dve.wait_ge(unit_out[U % 2], U // 2 + 1)
                            for h in range(HALVES):
                                cs = slice(n * BLK, (n + 1) * BLK)
                                ins = nc.vector.tensor_tensor(xw[:, h, cs], res[:, h, cs], fw[:, cs], ALU.mult)
                            ins.then_inc(xw_ready, 1)

            def mixer():
                for s in range(MU * GL):
                    split_at(T_MX + s + RING)
                    if s == 2:
                        turn_residual(HI_D1 + 2 * (UN - 1), C_MX, UN - 1)
                    if s == 4:
                        mean_square(N_MX)
                    if s == 5:
                        inverse(N_MX)
                    if s == GL + 1:
                        dve.wait_ge(mm_done, T_MX)
                        own(nc.vector.memset(probs[:], 0.0))
                    for g in range(GROUPS):
                        f, q, i, gt = (m_end(kind, g) for kind in "fqig")
                        if s == f + 5:
                            dve.wait_ge(lf_ready, g + 1)
                            if g == 0:
                                dve.wait_ge(consts, 8)
                            flat = "p a b -> p (a b)"
                            nc.vector.tensor_tensor_scan(bc[:].rearrange(flat), restart[:], lf[:].rearrange(flat), 0.0,
                                                         ALU.mult, ALU.add).then_inc(bc_ready, 1)
                            dve.wait_ge(bc_ready, 2 * g + 1)
                            by_chunk = bc[:].rearrange("p a (n c) -> p (a n) c", c=CHUNK)
                            nc.vector.tensor_tensor(kst[:].rearrange("p a (n c) -> p (a n) c", c=CHUNK),
                                                    by_chunk[:, :, CHUNK - 1:CHUNK].broadcast_to(by_chunk.shape), by_chunk,
                                                    ALU.subtract).then_inc(bc_ready, 1)
                        for dst, nth in ((kst, 0), (kdec, 1)):
                            if s == f + 8 + nth:
                                dve.wait_ge(exp_ready, 3 * g + nth + 1)
                                for j in range(NB):
                                    hd = g * NB + j
                                    ins = nc.vector.scalar_tensor_tensor(dst[:, j, :], kk[:, j, :], lbw[:, 7, hd:hd + 1],
                                                                         dst[:, j, :], ALU.mult, ALU.mult)
                                ins.then_inc(k_ready, 1)
                        if s == q + 3:
                            dve.wait_ge(turned, m_turn("q", g) + 1)
                            dve.wait_ge(exp_ready, 3 * g + 3)
                            for h in range(HALVES):
                                hs = slice(h * P, (h + 1) * P)
                                ins = nc.vector.tensor_tensor(qdec[:, :, hs], turn[h][:], eb[:, :, hs], ALU.mult)
                            ins.then_inc(turn_done, 1)
                        if s == q + 7:
                            dve.wait_ge(xb_full, xjob(g, X_SCORE))
                            for h in range(HALVES):
                                for j in range(NB):
                                    ins = nc.vector.copy_predicated(probs[:, h, j, :], causal[:].bitcast(U32),
                                                                    xb[h][:, j, :])
                            ins.then_inc(xb_done, 1)
                        if s == i + 2:
                            dve.wait_ge(xb_full, xjob(g, X_S12))
                            own(nc.vector.tensor_copy(state[:, 0], xb[0][:]))
                            for j in range(NB):
                                last = 2 * CHUNK - 1
                                ins = nc.vector.scalar_tensor_tensor(state[:, 1, j, :], state[:, 0, j, :],
                                                                     eb[:, j, last:last + 1], xb[1][:, j, :],
                                                                     ALU.mult, ALU.add)
                            ins.then_inc(xb_done, 1)
                        if s == i + 5:
                            dve.wait_ge(xb_full, xjob(g, X_S3))
                            for j in range(NB):
                                last = 3 * CHUNK - 1
                                ins = nc.vector.scalar_tensor_tensor(state[:, 2, j, :], state[:, 1, j, :],
                                                                     eb[:, j, last:last + 1], xb[0][:, j, :],
                                                                     ALU.mult, ALU.add)
                            ins.then_inc(xb_done, 1)
                        if s == i + 8:
                            dve.wait_ge(xb_full, xjob(g, X_O))
                            for h in range(HALVES):
                                ins = nc.vector.tensor_copy(osb[:, 2 * h:2 * h + 2, :].rearrange("p a b -> p (a b)"),
                                                            xb[h][:].rearrange("p a b -> p (a b)"))
                            ins.then_inc(xb_done, 1)
                        if s == gt + 5:
                            dve.wait_ge(rs_ready, g + 1)
                            for j in range(NB):
                                ins = nc.vector.scalar_tensor_tensor(osb[:, j, :], osb[:, j, :],
                                                                     cols[:, C_ON + g * NB + j:C_ON + g * NB + j + 1],
                                                                     lf[:, j, :], ALU.mult, ALU.mult)
                            ins.then_inc(on_ready, 1)
                        if s == gt + 6:
                            dve.wait_ge(on_ready, g + 1)
                            dve.wait_ge(turn_done, m_turn("g", g) + 1)
                            nc.vector.tensor_tensor(osb[:], osb[:], gsil[:], ALU.mult).then_inc(oa_ready, 1)
                        if s == gt + 8:
                            dve.wait_ge(oa_hi, g + 1)
                            nc.vector.tensor_tensor(h_lo[:, g * NB:(g + 1) * NB, :], osb[:],
                                                    h_hi[:, g * NB:(g + 1) * NB, :].bitcast(F32), ALU.subtract
                                                    ).then_inc(mixed, 1)
                        c, hh, b = (m_end(kind, g) for kind in "chb")
                        if s == hh + 3:
                            dve.wait_ge(turned, m_turn("h", g) + 1)
                            dve.wait_ge(turn_done, m_turn("c", g) + 1)
                            for h in range(HALVES):
                                hs = slice(h * P, (h + 1) * P)
                                ins = nc.vector.tensor_tensor(u_sb[:, :, hs], turn[h][:], c_sb[:, :, hs], ALU.mult)
                            ins.then_inc(turn_done, 1)
                        if s == hh + 4:
                            dve.wait_ge(turn_done, m_turn("h", g) + 1)
                            for back in range(3):
                                for j in range(NB):
                                    k = C_CV + (2 - back) * HEADS + g * NB + j
                                    w1 = cols[:, k:k + 1]
                                    if back == 0:
                                        ins = nc.vector.tensor_scalar(y_sb[:, j, :], u_sb[:, j, :], w1, None, ALU.mult)
                                    else:
                                        ins = nc.vector.scalar_tensor_tensor(
                                            y_sb[:, j, back:SEQ], u_sb[:, j, 0:SEQ - back], w1, y_sb[:, j, back:SEQ],
                                            ALU.mult, ALU.add)
                                own(ins)
                        if s == b + 3:
                            conv_out(g)
                        if s == b + 4:
                            conv_lo(g)

            def conv_out(g):
                dve.wait_ge(turned, m_turn("b", g) + 1)
                for h in range(HALVES):
                    hs = slice(h * P, (h + 1) * P)
                    ins = nc.vector.tensor_tensor(ob[:, :, hs], turn[h][:], y_sb[:, :, hs], ALU.mult)
                ins.then_inc(turn_done, 1)

            def conv_lo(g):
                dve.wait_ge(oa_hi, GROUPS + g + 1)
                ks = slice(HEADS + g * NB, HEADS + (g + 1) * NB)
                nc.vector.tensor_tensor(h_lo[:, ks, :], ob[:], h_hi[:, ks, :].bitcast(F32), ALU.subtract
                                        ).then_inc(mixed, 1)

            def other_columns():
                dve.wait_ge(cols_turned, 2)
                nc.vector.tensor_copy(cols[:, DK:NROWS], acc[1][1][:, DK:NROWS]).then_inc(cols_ready, 1)

            def lower_bounds():
                dve.wait_ge(cols_ready, 2)
                l0, l1 = cols[:, C_LB:C_LB + HEADS], cols[:, C_LB + HEADS:C_LB + 2 * HEADS]
                own(nc.vector.tensor_tensor(lbw[:, 0, :], l0, l1, ALU.max))
                nc.vector.tensor_tensor(lbw[:, 1, :], l0, lbw[:, 0, :], ALU.subtract)
                nc.vector.tensor_tensor(lbw[:, 2, :], l1, lbw[:, 0, :], ALU.subtract).then_inc(lb_in, 1)
                dve.wait_ge(lb_exp, 1)
                own(nc.vector.tensor_tensor(lbw[:, 0, :], lbw[:, 3, :], lbw[:, 4, :], ALU.add))
                own(nc.vector.reciprocal(lbw[:, 5, :], lbw[:, 0, :]))
                own(nc.vector.tensor_tensor(lbw[:, 6, :], lbw[:, 3, :], lbw[:, 5, :], ALU.mult))
                nc.vector.tensor_scalar(lbw[:, 7, :], lbw[:, 6, :], -1.0, 1.0, ALU.mult, ALU.add).then_inc(lb_ready, 1)

            nc.vector.memset(eps[:], EPS).then_inc(eps_set, 1)
            dve.wait_ge(cols_turned, 1)
            nc.vector.tensor_copy(cols[:, 0:DK], acc[1][0][:, 0:DK]).then_inc(cols_ready, 1)
            dve.wait_ge(cols_ready, 1)
            split_at(0)
            turn_residual(0, C_F1, 0)
            split_at(1)
            turn_residual(2, C_F1, 1, xb)
            split_at(2)
            split_at(3)
            HI_F1 = 2 * UN
            HI_D1 = HI_F1 + FU
            HI_OU = HI_D1 + 2 * UN
            HI_F2 = HI_OU + 2 * UN
            ffn(0, N_F1, T_F1, U_F1, HI_F1, None)
            lower_bounds()
            back_to_residual(DL, T_D1, U_D1, N_MX, 0.5, HI_D1, C_MX, lambda: turn_hidden(HI_D1 - 1, FU - 1))
            mixer()

            def conv_tail():
                conv_out(GROUPS - 1)
                conv_lo(GROUPS - 1)
            back_to_residual(GL, T_OU, U_OU, N_F2, 1.0, HI_OU, C_F2, conv_tail)
            ffn(1, N_F2, T_F2, U_F2, HI_F2, HI_OU + 2 * (UN - 1))
            back_to_residual(DL, T_D2, U_D2, N_END, 0.5, None, None, lambda: turn_hidden(HI_F2 + FU - 1, FU - 1))
            cs = slice((UN - 1) * BLK, UN * BLK)
            last = U_D2 + UN - 1

            def add_half(h):
                part = res[:, h, cs]
                nc.vector.scalar_tensor_tensor(part, acc[last % 2][h][:], 0.5, part, ALU.mult, ALU.add
                                               ).then_inc(sum_ready, 1)
                dve.wait_ge(sum_ready, h + 1)
                nc.vector.tensor_tensor(xw[:, h, cs], res[:, h, cs], fw[:, cs], ALU.mult).then_inc(xw_ready, 1)

            def mean_half(h):
                dve.wait_ge(ssq_ready, 1 + HALVES * UN * N_END + HALVES * (UN - 1) + h + 1)
                own(nc.vector.reduce_sum(ms[:, N_END, h:h + 1], ssq[:, N_END, h, :], mybir.AxisListType.X))
                nc.vector.tensor_scalar(ms[:, N_END, h:h + 1], ms[:, N_END, h:h + 1], 1.0 / D, EPS, ALU.mult, ALU.add
                                        ).then_inc(ms_ready, 1)

            def inverse_half(h):
                dve.wait_ge(sd_ready, N_END + 1 + h)
                nc.vector.reciprocal(rstd[:, N_END, h:h + 1], sd[:, N_END, h:h + 1]).then_inc(rstd_ready, 1)

            dve.wait_ge(half_done, 1)
            add_half(0)
            dve.wait_ge(mm_done, TILES)
            add_half(1)
            mean_half(0)
            mean_half(1)
            inverse_half(0)
            inverse_half(1)
            dve.wait_ge(rstd_ready, N_END + 1)
            dve.wait_ge(xw_ready, UN)
            for piece in range(PIECES):
                cs = slice(piece * D // PIECES, (piece + 1) * D // PIECES)
                nc.vector.tensor_scalar(xw[:, 0, cs], xw[:, 0, cs], rstd[:, N_END, 0:1], None, ALU.mult
                                        ).then_inc(y_ready[0], 1)

        @block.tensor
        def _(pe):
            def products(tile, slot, k0, pair, hi, lo, first, last, by_half=False):
                pe.wait_ge(lo_ready, tile + 1)
                order = [(t, h) for t in range(KB) for h in range(HALVES)]
                if by_half:
                    order = [(t, h) for h in range(HALVES) for t in range(KB)]
                for t, h in order:
                    xs = slice(h * P, (h + 1) * P)
                    k = k0 + t
                    one, end = first and t == 0, last and t == KB - 1
                    nc.tensor.matmul(acc[pair][h][:], hi[:, k, xs], whi[:, slot, t, :], start=one, stop=False)
                    nc.tensor.matmul(acc[pair][h][:], hi[:, k, xs], wlo[:, slot, t, :], start=False, stop=False)
                    ins = nc.tensor.matmul(acc[pair][h][:], lo[:, k, xs], whi[:, slot, t, :], start=False, stop=end)
                    if by_half and (t, h) == (KB - 1, 0):
                        ins.then_inc(half_done, 1)
                ins.then_inc(mm_done, 1)

            def turn_tokens(job, unit_pair, count, src):
                pe.wait_ge(turn_done, job)
                pe.wait_ge(unit_out[unit_pair], count)
                for h in range(HALVES):
                    for j in range(NB):
                        ins = nc.tensor.transpose(turn[h][:, j, :], src[:, h, j * P:(j + 1) * P], ident[:])
                ins.then_inc(turned, 1)

            def turn_residual(job, n, U=None, turn=turn):
                if job >= UN:
                    pe.wait_ge(turn_done, job)
                elif job >= 2:
                    pe.wait_ge(turn_done, job - 1)
                if U is None:
                    pe.wait_ge(x_landed[n], 16)
                else:
                    pe.wait_ge(unit_out[U % 2], U // 2 + 1)
                for j in range(NB):
                    for h in range(HALVES):
                        c = n * BLK + j * P
                        ins = nc.tensor.transpose(turn[j // 2][:, 2 * (j % 2) + h, :], res[:, h, c:c + P], ident[:])
                ins.then_inc(turned, 1)

            def ffn(which, tile0, unit0, job0):
                before = unit0 // 2
                if before > 0:
                    pe.wait_ge(unit_out[0], before)
                for s in range(GL):
                    if which == 0:
                        pe.wait_ge(x_pair if s % 2 == 0 else turn_done, s // 2 + 1)
                    if which == 1 and s == GL - 2:
                        pe.wait_ge(turn_done, J_F2)
                    products(tile0 + s, s % RING, KB * s, 0, x_hi, x_lo, s == 0, s == GL - 1)
                    if which == 0 and s in (1, 3):
                        n = (s + 3) // 2
                        turn_residual(n, n, None, (turn, xb)[n % 2])
                    if which == 0 and s == 5:
                        pe.wait_ge(rows_landed, 16 * 5)
                        nc.tensor.transpose(acc[1][1][:, 0:NROWS], rows[0:NROWS, :], ident[0:NROWS, 0:NROWS]
                                            ).then_inc(cols_turned, 1)
                    if which == 1 and s == 1:
                        turn_residual(J_F2 - 1, UN - 1, U_F2 - 1)
                if before > 0:
                    pe.wait_ge(unit_out[1], before)
                else:
                    pe.wait_ge(cols_ready, 2)
                with pe.Fori(0, FU - 1) as c:
                    for s in range(2 * GL):
                        if s == GL:
                            pe.wait_ge(unit_out[0], before + c + 1)
                        k = s % GL
                        products(tile0 + 2 * GL * c + GL + s, (GL + s) % RING, KB * k, 1 if s < GL else 0, x_hi, x_lo,
                                 k == 0, k == GL - 1)
                        if s == GL + 1:
                            turn_tokens(job0 + c, 1, before + c + 1, tm[:, 1])
                for s in range(GL):
                    products(tile0 + (2 * FU - 1) * GL + s, ((2 * FU - 1) * GL + s) % RING, KB * s, 1, x_hi, x_lo,
                             s == 0, s == GL - 1)

            def back_to_residual(tiles, tile0, unit0, job0, residual, first):
                for s in range(UN * tiles):
                    n, k = s // tiles, s % tiles
                    U = unit0 + n
                    if k == 0:
                        pe.wait_ge(unit_out[U % 2], U // 2)
                    if tiles == GL and n == 0 and k % 2 == 0:
                        pe.wait_ge(mixed, k // 2 + 1)
                    if tiles == DL and n == 0 and k == DL - 2:
                        pe.wait_ge(turn_done, job0)
                    products(tile0 + s, s % RING, KB * k, U % 2, h_hi, h_lo, k == 0, k == tiles - 1,
                             tile0 + s == TILES - 1)
                    if k == 1 and n == 0:
                        first()
                    if k == 1 and n > 0 and residual:
                        turn_residual(job0 + n - 1, n - 1, U - 1)

            def mixer():
                for s in range(MU * GL):
                    u, k = s // GL, s % GL
                    U = U_MX + u
                    if k == 0:
                        pe.wait_ge(unit_out[U % 2], U // 2)
                    if s == GL - 2:
                        pe.wait_ge(turn_done, J_MX)
                    products(T_MX + s, s % RING, KB * k, U % 2, x_hi, x_lo, k == 0, k == GL - 1)
                    if s == 1:
                        turn_residual(J_MX - 1, UN - 1, U_MX - 1)
                    for kind, g in TURNED:
                        if s == m_end(kind, g) + 2:
                            turn_mixed(kind, g)
                    for g in range(GROUPS):
                        f, q, i, gt = (m_end(kind, g) for kind in "fqig")
                        recurrence(s, g, f, q, i, gt)

            def turn_mixed(kind, g):
                U = U_MX + MIX.index((kind, g))
                turn_tokens(m_turn(kind, g), U % 2, U // 2 + 1, tm[:, TURNED.index((kind, g)) % 2])

            def recurrence(s, g, f, q, i, gt):
                if s == f + 12:
                    if g > 0:
                        pe.wait_ge(xb_done, xjob(g, X_KST) - 1)
                    pe.wait_ge(k_ready, 2 * g + 2)
                    for h in range(HALVES):
                        for j in range(NB):
                            ins = nc.tensor.transpose(xb[h][:, j, :], kst[:, j, h * P:(h + 1) * P], ident[:])
                    ins.then_inc(xb_full, 1)
                if s == q + 6:
                    pe.wait_ge(xb_done, xjob(g, X_SCORE) - 1)
                    pe.wait_ge(turn_done, m_turn("q", g) + 1)
                    for h in range(HALVES):
                        hs = slice(h * P, (h + 1) * P)
                        for j in range(NB):
                            ins = nc.tensor.matmul(xb[h][:, j, :], kdec[:, j, hs], qdec[:, j, hs], start=True, stop=True)
                    ins.then_inc(xb_full, 1)
                if s == i + 1:
                    pe.wait_ge(xb_done, xjob(g, X_S12) - 1)
                    U = U_MX + MIX.index(("i", g))
                    pe.wait_ge(unit_out[U % 2], U // 2 + 1)
                    for n in range(2):
                        ps = slice(n * CHUNK, (n + 1) * CHUNK)
                        for j in range(NB):
                            ins = nc.tensor.matmul(xb[n][:, j, :], kst_tm[ps, 0, j, :], v_tm[ps, 0, j * P:(j + 1) * P],
                                                   start=True, stop=True)
                    ins.then_inc(xb_full, 1)
                if s == i + 4:
                    pe.wait_ge(xb_done, xjob(g, X_S3) - 1)
                    for j in range(NB):
                        ins = nc.tensor.matmul(xb[0][:, j, :], kst_tm[0:CHUNK, 1, j, :], v_tm[0:CHUNK, 1, j * P:(j + 1) * P],
                                               start=True, stop=True)
                    ins.then_inc(xb_full, 1)
                if s == i + 7:
                    pe.wait_ge(xb_done, xjob(g, X_O) - 1)
                    for j in range(NB):
                        flat = xb[j // 2][:].rearrange("p a b -> p (a b)")
                        for h in range(HALVES):
                            at0 = (j % 2) * SEQ + h * P
                            nc.tensor.matmul(flat[:, at0:at0 + P], v_tm[:, h, j * P:(j + 1) * P], probs[:, h, j, :],
                                             start=True, stop=False)
                            for n in range(max(2 * h, 1), 2 * h + 2):
                                at0 = (j % 2) * SEQ + n * CHUNK
                                ins = nc.tensor.matmul(flat[:, at0:at0 + CHUNK], state[:, n - 1, j, :],
                                                       qdec[:, j, n * CHUNK:(n + 1) * CHUNK], start=False, stop=(n % 2 == 1))
                    ins.then_inc(xb_full, 1)
                if s == gt + 2:
                    pe.wait_ge(consts, 3)
                    pe.wait_ge(xb_done, xjob(g, X_NORM) - 1)
                    pe.wait_ge(osq_ready, g + 1)
                    for h in range(HALVES):
                        ins = nc.tensor.matmul(xb[h][:].rearrange("p a b -> p (a b)"), ones[:],
                                               kk[:, 2 * h:2 * h + 2, :].rearrange("p a b -> p (a b)"),
                                               start=True, stop=True)
                    ins.then_inc(xb_full, 1)

            WARM = (4, 2, 8)

            def warm(count):
                for _ in range(count):
                    nc.tensor.matmul(acc[0][1][:, 0:P], ident[:], ident[:], start=True, stop=True).then_inc(warmed, 1)

            pe.wait_ge(consts, 2)
            warm(WARM[0])
            pe.wait_ge(gain_landed, 16)
            nc.tensor.transpose(acc[1][0][:, 0:DK], rows[0:DK, :], ident[0:DK, 0:DK]).then_inc(cols_turned, 1)
            warm(WARM[1])
            turn_residual(0, 0)
            warm(WARM[2])
            turn_residual(1, 1, None, xb)
            pe.wait_ge(warmed, sum(WARM))
            ffn(0, T_F1, U_F1, J_F1)
            back_to_residual(DL, T_D1, U_D1, J_D1, True,
                             lambda: turn_tokens(J_D1 - 1, 1, U_D1 // 2, tm[:, 1]))
            mixer()
            back_to_residual(GL, T_OU, U_OU, J_OU, True, lambda: turn_mixed("b", GROUPS - 1))
            ffn(1, T_F2, U_F2, J_F2)
            back_to_residual(DL, T_D2, U_D2, J_F2 + FU, False,
                             lambda: turn_tokens(J_F2 + FU - 1, 1, U_D2 // 2, tm[:, 1]))


_INS = ["x", "ffn1_norm_w", "ffn1_w_gate", "ffn1_w_up", "ffn1_w_down", "mix_norm_w", "w_in_mix", "hgrn_lb_logits",
        "hgrn_out_norm_w", "conv_w", "w_out_mix", "ffn2_norm_w", "ffn2_w_gate", "ffn2_w_up", "ffn2_w_down",
        "final_norm_w"]


def kernel(**inputs):
    import numpy as _np
    import concourse.bacc as _bacc
    from concourse import mybir as _mybir
    from concourse.bass_utils import run_bass_kernel_spmd as _run

    nc = _bacc.Bacc("TRN2", target_bir_lowering=False, num_devices=1)
    arrays, args = {}, []
    for name in _INS:
        a = _np.ascontiguousarray(inputs[name])
        arrays[f"in_{name}_dram"] = a
        args.append(nc.dram_tensor(f"in_{name}_dram", a.shape, _mybir.dt.from_np(a.dtype), kind="ExternalInput").ap())
    args.append(nc.dram_tensor("out_0_dram", inputs["x"].shape, _mybir.dt.float32, kind="ExternalOutput").ap())
    build(nc, *args)
    r = _run(nc, [arrays], core_ids=[0])
    return r.results[0]["out_0_dram"]
```
